# Optimizing a Trainium2 kernel written in Bass

```python
import math
import jax, jax.numpy as jnp
from jax import lax
import numpy as np

D_MODEL = 1024
BATCH = 1
SEQ = 512
DEPTH = 2

DIFF_HEADS = 4
DIFF_HD = 64
DIFF_W = DIFF_HEADS * 2 * DIFF_HD
MLA_HEADS = 8
MLA_NOPE = 64
MLA_ROPE = 32
MLA_V = 64
MLA_QK = MLA_NOPE + MLA_ROPE
Q_LORA = 256
KV_LORA = 128
MLA_W = MLA_HEADS * MLA_V
ROPE_THETA = 10000.0
CONV_W = 512
CONV_K = 3
N_BRANCH = 3
PEER_HEADS = 8
N_KEYS = 128
N_EXPERTS = N_KEYS * N_KEYS
PEER_DQ = 256
PEER_DK = PEER_DQ // 2
K_SUB = 16
PEER_TOPK = 16
PEER_CHUNK = 128
PLE_DIM = 256
BLOCK_Q = 128
NORM_EPS = 1e-6
NEG_INF = -1e30
IN_SPLITS = (DIFF_W, DIFF_W, DIFF_W, Q_LORA, KV_LORA, MLA_ROPE, CONV_W, CONV_W, CONV_W, N_BRANCH * D_MODEL)
D_IN = 3 * DIFF_W + Q_LORA + KV_LORA + MLA_ROPE + 3 * CONV_W + N_BRANCH * D_MODEL

kernel_name = "hybrid_diffattn_mla_shortconv_peer"

def _rms(x, g):
    xf = x.astype(jnp.float32)
    y = xf * lax.rsqrt(jnp.mean(xf * xf, axis=-1, keepdims=True) + NORM_EPS)
    return (y * g.astype(jnp.float32)).astype(x.dtype)

def _alibi_slopes(n):
    return 2.0 ** (-8.0 * jnp.arange(1, n + 1, dtype=jnp.float32) / n)

def _rope(x, pos):
    half = MLA_ROPE // 2
    freqs = ROPE_THETA ** (-jnp.arange(half, dtype=jnp.float32) / half)
    ang = pos.astype(jnp.float32)[:, None] * freqs[None, :]
    cos, sin = jnp.cos(ang), jnp.sin(ang)
    x1 = x[..., :half].astype(jnp.float32)
    x2 = x[..., half:].astype(jnp.float32)
    out = jnp.concatenate([x1 * cos - x2 * sin, x2 * cos + x1 * sin], axis=-1)
    return out.astype(x.dtype)

def _causal_probs(qb, k, start, scale, slopes):
    nq, nk = qb.shape[-2], k.shape[-2]
    s = jnp.einsum('bhmqd,bhmkd->bhmqk', qb, k).astype(jnp.float32) * scale
    dist = (start + jnp.arange(nq))[:, None] - jnp.arange(nk)[None, :]
    if slopes is not None:
        s = s - slopes[None, :, None, None, None] * jnp.abs(dist).astype(jnp.float32)
    s = jnp.where(dist >= 0, s, NEG_INF)
    return jax.nn.softmax(s, axis=-1)

def _sweep_blocks(block_fn, seq):
    out = lax.map(block_fn, jnp.arange(seq // BLOCK_Q))
    out = jnp.moveaxis(out, 0, 2)
    return out.reshape(out.shape[0], out.shape[1], seq, out.shape[-1])

def _diff_attention(q_raw, k_raw, v_raw, g_q, g_k, lq1, lk1, lq2, lk2, g_sub, lambda_init):
    B, S, _ = q_raw.shape
    q = _rms(q_raw.reshape(B, S, DIFF_HEADS, 2, DIFF_HD), g_q).transpose(0, 2, 3, 1, 4)
    k = _rms(k_raw.reshape(B, S, DIFF_HEADS, 2, DIFF_HD), g_k).transpose(0, 2, 3, 1, 4)
    v = v_raw.reshape(B, S, DIFF_HEADS, 2 * DIFF_HD).transpose(0, 2, 1, 3)
    lam = (jnp.exp(jnp.sum(lq1.astype(jnp.float32) * lk1.astype(jnp.float32)))
           - jnp.exp(jnp.sum(lq2.astype(jnp.float32) * lk2.astype(jnp.float32)))
           + lambda_init)
    slopes = _alibi_slopes(DIFF_HEADS)
    scale = DIFF_HD ** -0.5

    def block(i):
        start = i * BLOCK_Q
        qb = lax.dynamic_slice_in_dim(q, start, BLOCK_Q, axis=3)
        p = _causal_probs(qb, k, start, scale, slopes)
        a = p[:, :, 0] - lam * p[:, :, 1]
        return jnp.einsum('bhqk,bhkd->bhqd', a.astype(v.dtype), v)

    o = _sweep_blocks(block, S)
    o = _rms(o, g_sub) * (1.0 - lambda_init)
    return o.transpose(0, 2, 1, 3).reshape(B, S, DIFF_W)

def _mla(c_q, c_kv, k_rope, g_cq, w_uq, g_ckv, w_ukv, g_q, g_k):
    B, S, _ = c_q.shape
    pos = jnp.arange(S)
    q = (_rms(c_q, g_cq) @ w_uq).reshape(B, S, MLA_HEADS, MLA_QK)
    kv = (_rms(c_kv, g_ckv) @ w_ukv).reshape(B, S, MLA_HEADS, MLA_NOPE + MLA_V)
    k_nope, v = kv[..., :MLA_NOPE], kv[..., MLA_NOPE:]
    k = jnp.concatenate([k_nope, jnp.broadcast_to(k_rope[:, :, None, :], (B, S, MLA_HEADS, MLA_ROPE))], axis=-1)
    q = _rms(q, g_q).transpose(0, 2, 1, 3)
    k = _rms(k, g_k).transpose(0, 2, 1, 3)
    q = jnp.concatenate([q[..., :MLA_NOPE], _rope(q[..., MLA_NOPE:], pos)], axis=-1)[:, :, None]
    k = jnp.concatenate([k[..., :MLA_NOPE], _rope(k[..., MLA_NOPE:], pos)], axis=-1)[:, :, None]
    v = v.transpose(0, 2, 1, 3)
    scale = MLA_QK ** -0.5

    def block(i):
        start = i * BLOCK_Q
        qb = lax.dynamic_slice_in_dim(q, start, BLOCK_Q, axis=3)
        p = _causal_probs(qb, k, start, scale, None)[:, :, 0]
        return jnp.einsum('bhqk,bhkd->bhqd', p.astype(v.dtype), v)

    o = _sweep_blocks(block, S)
    return o.transpose(0, 2, 1, 3).reshape(B, S, MLA_W)

def _short_conv(b_gate, c_gate, xv, conv_w):
    u = c_gate * xv
    S = u.shape[1]
    up = jnp.pad(u, ((0, 0), (CONV_K - 1, 0), (0, 0)))
    y = conv_w[0] * up[:, 0:S]
    for j in range(1, CONV_K):
        y = y + conv_w[j] * up[:, j:j + S]
    return b_gate * y

def _peer(h, w_query, sub_keys, u_tab, v_tab):
    B, S, D = h.shape
    ht = h.reshape(-1, PEER_CHUNK, D)

    def chunk(hc):
        T = hc.shape[0]
        q = (hc @ w_query).reshape(T, PEER_HEADS, 2, PEER_DK)
        s = jnp.einsum('thpd,phnd->thpn', q, sub_keys).astype(jnp.float32)
        top_s, top_i = lax.top_k(s, K_SUB)
        cand = (top_s[:, :, 0, :, None] + top_s[:, :, 1, None, :]).reshape(T, PEER_HEADS, K_SUB * K_SUB)
        best_s, best_c = lax.top_k(cand, PEER_TOPK)
        i1 = jnp.take_along_axis(top_i[:, :, 0], best_c // K_SUB, axis=-1)
        i2 = jnp.take_along_axis(top_i[:, :, 1], best_c % K_SUB, axis=-1)
        expert = i1 * N_KEYS + i2
        gate = jax.nn.softmax(best_s, axis=-1)
        u_sel = u_tab[expert]
        act = jax.nn.gelu(jnp.einsum('thkd,td->thk', u_sel, hc), approximate=False)
        w = (gate * act.astype(jnp.float32)).astype(hc.dtype)
        return jnp.einsum('thk,thkd->td', w, v_tab[expert])

    return lax.map(chunk, ht).reshape(B, S, D)

def _layer(x, p_i, layer_idx, g_mix, w_in, g_diff_q, g_diff_k, lam_q1, lam_k1, lam_q2, lam_k2,
           g_diff_sub, g_cq, w_uq, g_ckv, w_ukv, g_mla_q, g_mla_k, conv_w, w_br_diff, w_br_mla,
           w_br_conv, w_out, g_ffn, w_query, sub_keys, u_experts, v_experts, g_ple, w_ple_gate,
           w_ple_proj):
    B, S, D = x.shape
    lambda_init = 0.8 - 0.6 * math.exp(-0.3 * layer_idx)
    h = _rms(x, g_mix)
    z = h @ w_in
    offsets = np.cumsum(IN_SPLITS)[:-1].tolist()
    dq, dk, dv, cq, ckv, kr, cb, cc, cx, gates = jnp.split(z, offsets, axis=-1)
    y_d = _diff_attention(dq, dk, dv, g_diff_q, g_diff_k, lam_q1, lam_k1, lam_q2, lam_k2, g_diff_sub, lambda_init)
    y_m = _mla(cq, ckv, kr, g_cq, w_uq, g_ckv, w_ukv, g_mla_q, g_mla_k)
    y_c = _short_conv(cb, cc, cx, conv_w)
    g = jax.nn.sigmoid(gates).reshape(B, S, N_BRANCH, D)
    mixed = g[:, :, 0] * (y_d @ w_br_diff) + g[:, :, 1] * (y_m @ w_br_mla) + g[:, :, 2] * (y_c @ w_br_conv)
    x = x + mixed @ w_out
    x = x + _peer(_rms(x, g_ffn), w_query, sub_keys, u_experts, v_experts)
    x = x + jax.nn.sigmoid(_rms(x, g_ple) @ w_ple_gate) * (p_i @ w_ple_proj)
    return x

def setup_inputs(seed: int = 0) -> dict:
    key = jax.random.key(seed)
    ks = jax.random.split(key, 30)
    L, D = DEPTH, D_MODEL

    def nrm(k, shape, scale):
        return jax.random.normal(k, shape, jnp.float32) * scale

    def gain(k, shape):
        return 1.0 + 0.05 * jax.random.normal(k, shape, jnp.float32)

    return {
        "x": nrm(ks[0], (BATCH, SEQ, D), 1.0),
        "p": nrm(ks[1], (DEPTH, BATCH, SEQ, PLE_DIM), 1.0),
        "g_mix": gain(ks[2], (L, D)),
        "w_in": nrm(ks[3], (L, D, D_IN), D ** -0.5),
        "g_diff_q": gain(ks[4], (L, DIFF_HD)),
        "g_diff_k": gain(ks[5], (L, DIFF_HD)),
        "lam_q1": nrm(ks[6], (L, DIFF_HD), 0.1),
        "lam_k1": nrm(ks[7], (L, DIFF_HD), 0.1),
        "lam_q2": nrm(ks[8], (L, DIFF_HD), 0.1),
        "lam_k2": nrm(ks[9], (L, DIFF_HD), 0.1),
        "g_diff_sub": gain(ks[10], (L, 2 * DIFF_HD)),
        "g_cq": gain(ks[11], (L, Q_LORA)),
        "w_uq": nrm(ks[12], (L, Q_LORA, MLA_HEADS * MLA_QK), Q_LORA ** -0.5),
        "g_ckv": gain(ks[13], (L, KV_LORA)),
        "w_ukv": nrm(ks[14], (L, KV_LORA, MLA_HEADS * (MLA_NOPE + MLA_V)), KV_LORA ** -0.5),
        "g_mla_q": gain(ks[15], (L, MLA_QK)),
        "g_mla_k": gain(ks[16], (L, MLA_QK)),
        "conv_w": nrm(ks[17], (L, CONV_K, CONV_W), CONV_K ** -0.5),
        "w_br_diff": nrm(ks[18], (L, DIFF_W, D), DIFF_W ** -0.5),
        "w_br_mla": nrm(ks[19], (L, MLA_W, D), MLA_W ** -0.5),
        "w_br_conv": nrm(ks[20], (L, CONV_W, D), CONV_W ** -0.5),
        "w_out": nrm(ks[21], (L, D, D), D ** -0.5),
        "g_ffn": gain(ks[22], (L, D)),
        "w_query": nrm(ks[23], (L, D, PEER_HEADS * PEER_DQ), D ** -0.5),
        "sub_keys": nrm(ks[24], (L, 2, PEER_HEADS, N_KEYS, PEER_DK), PEER_DK ** -0.5),
        "u_experts": nrm(ks[25], (L, N_EXPERTS, D), D ** -0.5),
        "v_experts": nrm(ks[26], (L, N_EXPERTS, D), PEER_HEADS ** -0.5),
        "g_ple": gain(ks[27], (L, D)),
        "w_ple_gate": nrm(ks[28], (L, D, D), D ** -0.5),
        "w_ple_proj": nrm(ks[29], (L, PLE_DIM, D), PLE_DIM ** -0.5),
    }

def reference(x, p, g_mix, w_in, g_diff_q, g_diff_k, lam_q1, lam_k1, lam_q2, lam_k2, g_diff_sub,
              g_cq, w_uq, g_ckv, w_ukv, g_mla_q, g_mla_k, conv_w, w_br_diff, w_br_mla, w_br_conv,
              w_out, g_ffn, w_query, sub_keys, u_experts, v_experts, g_ple, w_ple_gate, w_ple_proj):
    for i in range(DEPTH):
        x = _layer(x, p[i], i, g_mix[i], w_in[i], g_diff_q[i], g_diff_k[i], lam_q1[i], lam_k1[i],
                   lam_q2[i], lam_k2[i], g_diff_sub[i], g_cq[i], w_uq[i], g_ckv[i], w_ukv[i],
                   g_mla_q[i], g_mla_k[i], conv_w[i], w_br_diff[i], w_br_mla[i], w_br_conv[i],
                   w_out[i], g_ffn[i], w_query[i], sub_keys[i], u_experts[i], v_experts[i],
                   g_ple[i], w_ple_gate[i], w_ple_proj[i])
    return x


_drawn_inputs = setup_inputs


def setup_inputs(seed=0):
    import zlib

    import numpy as np

    out = dict(_drawn_inputs(seed))
    spreads = {}
    factors = {'g_cq': 3.529,
     'g_ckv': 2.713,
     'g_mla_q': 3.8,
     'g_mla_k': 3.265,
     'g_ple': 3.558,
     'lam_q2': 3.579}
    for name, (base, spread) in spreads.items():
        noise = np.random.default_rng([zlib.crc32(name.encode()), seed]).standard_normal(out[name].shape)
        drawn = base * np.exp(spread * noise) if base else spread * noise
        out[name] = __import__('jax').numpy.asarray(drawn.astype(out[name].dtype))
    for name, factor in factors.items():
        out[name] = (out[name] * factor).astype(out[name].dtype)
    return out
```

```python
from contextlib import ExitStack

import numpy as np

import concourse.bass as bass
from concourse import mybir

F32 = mybir.dt.float32
U32 = mybir.dt.uint32
ALU = mybir.AluOpType
ACT = mybir.ActivationFunctionType
AX = mybir.AxisListType.X

P = 128
D = 1024
SEQ = 512
DEPTH = 2
KT = D // P
HALF = 256
STEPS = DEPTH * SEQ // HALF
EPS = 1e-6
MASKED = -1e30
LOWEST = -3e38
DH, DHD = 4, 64
MH, MQK, MNOPE, MROPE, MV = 8, 96, 64, 32, 64
QL, KVL = 256, 128
LATENT = QL + KVL + MROPE
HEADS, TOPK = 8, 16
HP = 2 * HEADS
ROWS = HEADS * TOPK
LAMBDA_INIT = [0.8 - 0.6 * float(np.exp(-0.3 * layer)) for layer in range(DEPTH)]
SLOPES = [2.0 ** (-8.0 * (h + 1) / DH) for h in range(DH)]

RING = 8
V_BY_DVE = 2
V_BY_PE = RING - V_BY_DVE
GROUPS = ROWS // RING
PHASES = ["U", "V", "U", "V"]

COLS = ["g_mix", "g_ple", "g_dq", "g_dk", "g_dsub", "g_cq", "g_ckv", "conv"]
COL_N = dict(g_mix=KT, g_ple=KT, g_dq=1, g_dk=1, g_dsub=1, g_cq=2, g_ckv=1, conv=12)
COL_AT, NCOL = {}, 0
for _name in COLS:
    COL_AT[_name] = NCOL
    NCOL += COL_N[_name]

W_SLOTS = 3
PLE_TILES = [2048, 2048, 1024] * 2
MIX_TILES = [2048] * 18
DENSE_TILES = ([2048] * 6 + [2048] * 2 + [2048] * 6 + [1536, 1024] + MIX_TILES + [2048] * 4
               + [2048] * 8 + [2048])
NT_PLE, NT_DENSE = len(PLE_TILES), len(DENSE_TILES)

COUNTS = {
    "ple_norm": (8, 3, 0, 4), "ple_out": (2, 0, 2, 2),
    "x_norm": (8, 3, 0, 4), "qkv": (2, 0, 0, 0), "latent": (2, 0, 0, 0),
    "conv_c": (2, 0, 0, 0), "conv_x": (0, 0, 2, 0), "conv_b": (2, 0, 0, 0), "taps": (0, 0, 0, 15),
    "diff_norm": (0, 1, 0, 5), "diff_turn": (8, 0, 0, 0),
    "diff_scores": (0, 2, 2, 2), "diff_apply": (2, 0, 0, 4), "diff_sub": (1, 1, 0, 5),
    "mla_norm": (3, 5, 0, 5), "mla_up": (8, 4, 0, 0), "mla_qk": (0, 1, 0, 28), "mla_turn": (16, 0, 0, 0),
    "mla_scores": (0, 1, 1, 1), "mla_apply": (2, 0, 0, 1), "mla_out": (1, 0, 0, 0),
    "mix_first": (2, 0, 2, 0), "mix_more": (2, 0, 2, 2), "mix_turn": (8, 0, 0, 0), "out": (0, 0, 2, 0),
    "ffn_norm": (8, 3, 0, 4), "query": (2, 0, 0, 0), "scores": (4, 0, 0, 0),
    "topk": (0, 1, 0, 135),
}
COST = {
    "ple_norm": 12, "ple_out": 18, "x_norm": 12, "qkv": 14, "latent": 12, "conv_c": 7, "conv_x": 7,
    "conv_b": 7, "taps": 9, "diff_norm": 9, "diff_turn": 4, "diff_scores": 3, "diff_apply": 2,
    "diff_sub": 3, "mla_norm": 5, "mla_up": 9, "mla_qk": 18, "mla_turn": 6, "mla_scores": 1.5,
    "mla_apply": 1.5, "mla_out": 1, "mix_first": 21, "mix_more": 21, "mix_turn": 4, "out": 14,
    "ffn_norm": 12, "query": 7, "scores": 4, "topk": 50,
}
U_SHARE = 0.72


class At:

    def __init__(self, base, tiles):
        self.evacs, self.act, self.taken, self.dve = base
        self.tile = tiles


def tiles_done(name, at, pairs):
    if name in ("ple_out", "mix_first", "mix_more"):
        return [("w_used", pairs + 1), ("for_act", at.evacs + 2), ("for_dve", at.taken + 2)]
    if name in ("qkv", "latent"):
        return [("w_used", pairs + 1), ("for_act", at.evacs + 2)]
    if name == "out":
        return [("w_used", pairs + 1), ("for_dve", at.taken + 2)]
    if name == "mla_up":
        return [("for_act", at.evacs + 8)] * 2
    if name == "conv_x":
        return [("for_dve", at.taken + 2)]
    if name in ("conv_c", "conv_b", "query"):
        return [("for_act", at.evacs + 2)]
    return [("for_act", at.evacs + 4)]


def stages_of(step):
    out = []
    done = step - 1
    if done >= 0:
        out += [("ple_norm", done)] + [("ple_out", done, n) for n in range(2)]
    d = step + 1
    if d < STEPS:
        out += [("x_norm", d)] + [("qkv", d, n) for n in range(3)] + [("latent", d)]
        out += [("conv_c", d, 0), ("conv_c", d, 1), ("conv_x", d, 0), ("conv_x", d, 1),
                ("conv_b", d, 0), ("conv_b", d, 1), ("taps", d)]
        out += [("diff_norm", d), ("diff_turn", d)]
        heads = [(t, h) for t in range(2) for h in range(DH)]
        for i, (t, h) in enumerate(heads):
            out.append(("diff_scores", d, t, h))
            if i:
                out.append(("diff_apply", d, *heads[i - 1]))
        out.append(("diff_apply", d, *heads[-1]))
        out += [("diff_sub", d, t) for t in range(2)]
        out += [("mla_norm", d), ("mla_up", d), ("mla_qk", d), ("mla_turn", d)]
        heads = [(t, h) for t in range(2) for h in range(MH)]
        for i, (t, h) in enumerate(heads):
            out.append(("mla_scores", d, t, h))
            if i:
                out.append(("mla_apply", d, *heads[i - 1]))
        out.append(("mla_apply", d, *heads[-1]))
        out += [("mla_out", d, t) for t in range(2)]
        for n in range(2):
            out += [("mix_first", d, n, 0), ("mix_more", d, n, 1), ("mix_more", d, n, 2)]
        out += [("mix_turn", d), ("out", d, 0), ("out", d, 1), ("ffn_norm", d)]
        out += [("query", d, i) for i in range(HP // 2)]
        out += [("scores", d, 0), ("topk", d, 0), ("scores", d, 1), ("topk", d, 1)]
    return out


TILES_OF = {"ple_out": 3, "qkv": 2, "latent": 2, "conv_c": 1, "conv_x": 1, "conv_b": 1, "mla_up": 2,
            "mix_first": 3, "mix_more": 3, "out": 2, "query": 1}


def timeline():
    base, tile, plan, where, done, pairs = [0, 0, 0, 0], 0, [], {}, [], 0
    for step in range(-1, STEPS + 1):
        row, spent, served = [], 0.0, 0
        stages = stages_of(step)
        whole = sum(COST[st[0]] for st in stages)
        for st in stages:
            at = At(tuple(base), tile)
            where[st] = at
            base = [a + b for a, b in zip(base, COUNTS[st[0]])]
            tiles = TILES_OF.get(st[0], 0) + (st[0] == "scores" and st[2] == 1)
            if tiles:
                tile += tiles
                done += tiles_done(st[0], at, pairs)
                pairs = max([n for name, n in done if name == "w_used"], default=0)
            spent += COST[st[0]]
            groups = 0
            if 0 <= step < STEPS:
                share, per = spent / whole, [U_SHARE / 2, (1 - U_SHARE) / 2] * 2
                want, phase = 0.0, 0
                while phase < 4 and share > 1e-9:
                    part = min(share, per[phase])
                    want += part / per[phase] * GROUPS
                    share -= part
                    phase += 1
                goal = min(int(want), 4 * GROUPS)
                if st[0] == "out" and st[2] == 1:
                    goal = max(goal, 3 * GROUPS)
                groups = max(0, goal - served)
                served += groups
            row.append((st, at, groups))
        plan.append((step, row, 4 * GROUPS - served if 0 <= step < STEPS else 0))
    return plan, where, done


PLAN, WHERE, TILE_DONE = timeline()


class Rows:

    def __init__(self):
        self.step, self.pos = -1, 0

    def parts(self, n):
        while n:
            phase, first = divmod(self.pos, GROUPS)
            m = min(n, GROUPS - first)
            yield phase, first, m
            self.pos += m
            n -= m


def dve_rows_before(step, phase):
    per = [ROWS, GROUPS * V_BY_DVE] * 2
    return step * sum(per) + sum(per[:phase])


def pe_rows_before(step, phase):
    per = [0, GROUPS * V_BY_PE] * 2
    return step * sum(per) + sum(per[:phase])


def turns_before(step, phase):
    return (step * 4 + phase) * GROUPS


def trunk(nc, a):
    ctx = ExitStack()
    with ctx:
        def sb(name, shape, dt=F32):
            return ctx.enter_context(nc.sbuf_tensor(name, shape, dt))

        def sem(name):
            return ctx.enter_context(nc.semaphore(name))

        x = sb("x", [P, 4, D])
        diff_v = sb("diff_v", [P, 4, 512])
        diff_kT = sb("diff_kT", [P, DH, SEQ])
        mla_kT = sb("mla_kT", [P, MH, SEQ])
        mla_v = sb("mla_v", [P, 4, 512])
        h_ffn = sb("h_ffn", [P, 2, D])
        ring = sb("ring", [P, RING, D])
        wt = sb("wt", [P, W_SLOTS, 2048])
        dist = sb("dist", [P, 512])
        mask = sb("mask", [P, 512])
        ident = sb("ident", [P, P])
        diag = sb("diag", [P, V_BY_PE, P])
        cols = sb("cols", [P, DEPTH, NCOL])
        ffn_row = sb("ffn_row", [P, D])
        mla_rows = sb("mla_rows", [P, DEPTH, 2, MQK])
        rope_cos = sb("rope_cos", [P, 4, MROPE])
        rope_sin = sb("rope_sin", [P, 4, MROPE])
        iota = sb("iota", [P, TOPK])
        pT = sb("pT", [P, 2, HALF])
        experts = sb("experts", [P, 2, 2, ROWS], U32)
        gate = sb("gate", [P, 2, 2, ROWS])
        staged = sb("staged", [P, 2, RING], U32)
        dots = sb("dots", [P, ROWS])
        weight = sb("weight", [P, ROWS])
        tail = sb("tail", [P, 4, 2])
        lam = sb("lam", [P, DEPTH, 4])
        dq_gain = sb("dq_gain", [P, DEPTH])
        dsub_gain = sb("dsub_gain", [P, DEPTH])
        stats = sb("stats", [P, 128])
        scratch = sb("scratch", [P, 512])

        area_h = sb("area_h", [P, 2048])
        area_b = sb("area_b", [P, 5120])
        area_e = sb("area_e", [P, 2048])
        area_f = sb("area_f", [P, 1024])
        area_y = sb("area_y", [P, 2, 512])
        area_t = sb("area_t", [P, 3072])
        latent = sb("latent", [P, 2, LATENT])

        hT = area_h[:, :].rearrange("p (k t) -> p k t", k=KT)
        normed = area_b[:, 0:2048].rearrange("p (t n) -> p t n", t=2)
        z = area_b[:, 0:2048].rearrange("p (c t n) -> p c t n", c=2, t=2)
        qm = area_b[:, 0:1536].rearrange("p (t h d) -> p t h d", t=2, h=MH)
        km = area_b[:, 1536:3072].rearrange("p (t h d) -> p t h d", t=2, h=MH)
        diff_qT = area_b[:, 3072:4096].rearrange("p (h t) -> p h t", h=DH)
        mla_qT = area_b[:, 3072:5120].rearrange("p (h t) -> p h t", h=MH)
        mixed = normed
        mixedT = area_b[:, 3072:5120].rearrange("p (k t) -> p k t", k=KT)
        queryT = area_b[:, 0:4096].rearrange("p (c t) -> p c t", c=HP)
        squares = area_e[:, :]
        conv_cT = area_e[:, 0:1024].rearrange("p (c t) -> p c t", c=4)
        conv_bT = area_e[:, 1024:2048].rearrange("p (c t) -> p c t", c=4)
        prob = area_e[:, :].rearrange("p (b m k) -> p b m k", b=2, m=2)
        gates = area_e[:, :].rearrange("p (b t n) -> p b t n", b=2, t=2)
        key_scores = area_e[:, :].rearrange("p (c n) -> p c n", c=HP)
        cqT = area_f[:, 0:512].rearrange("p (k t) -> p k t", k=2)
        ckvT = area_f[:, 512:768]
        probT = area_f[:, :].rearrange("p (b k q) -> p b k q", b=2, q=P)
        product = area_f[:, :].rearrange("p (t n) -> p t n", t=2)
        ydT = area_t[:, 0:1024].rearrange("p (k t) -> p k t", k=4)
        ymT = area_t[:, 1024:2048].rearrange("p (k t) -> p k t", k=4)
        ycT = area_t[:, 2048:3072].rearrange("p (k t) -> p k t", k=4)
        conv_u = area_t[:, 0:4 * (HALF + 2)].rearrange("p (k t) -> p k t", k=4)
        cand = area_t[:, 0:2048]
        top_v = area_h[:, 0:256].rearrange("p (c k) -> p c k", c=HP)
        top_i = area_h[:, 256:512].bitcast(U32).rearrange("p (c k) -> p c k", c=HP)
        top_f = area_h[:, 512:768].rearrange("p (h c k) -> p h c k", h=HEADS, c=2)
        best_v = area_h[:, 768:896].rearrange("p (h k) -> p h k", h=HEADS)
        best_c = area_h[:, 896:1024].bitcast(U32).rearrange("p (h k) -> p h k", h=HEADS)
        part_u = area_h[:, 1024:1280].bitcast(U32).rearrange("p (c k) -> p c k", c=2)
        part_f = area_h[:, 1280:1536].rearrange("p (c h k) -> p c h k", c=2, h=HEADS)
        part_i = area_h[:, 1536:1792].rearrange("p (c k) -> p c k", c=2)
        exps = area_h[:, 1792:1920].rearrange("p (h k) -> p h k", h=HEADS)
        lam_in = area_b[:, 4096:4096 + 4 * DHD * DEPTH].rearrange("p (l c d) -> p l c d", l=DEPTH, c=4)
        ss = stats[:, 0:32]
        mean_sq = stats[:, 32:64]
        root = stats[:, 64:96]
        top = stats[:, 96:100].rearrange("p (b m) -> p b m", b=2)
        neg_top = stats[:, 100:104].rearrange("p (b m) -> p b m", b=2)
        total = stats[:, 104:108].rearrange("p (b m) -> p b m", b=2)
        inv = stats[:, 108:112].rearrange("p (b m) -> p b m", b=2)
        rstd = sb("rstd", [P, 32])
        inv_lam = stats[:, 112:114]
        esum = stats[:, 114:122]
        ss_rope = stats[:, 122:124]

        ps_act = ctx.enter_context(nc.psum_tensor("ps_act", [P, 3, 512], F32))
        ps_dve = ctx.enter_context(nc.psum_tensor("ps_dve", [P, 3, 512], F32))
        ps_sum = ctx.enter_context(nc.psum_tensor("ps_sum", [P, 2, 512], F32))

        consts_loaded = sem("consts_loaded")
        x_loaded = [sem(f"x_loaded{i}") for i in range(2)]
        dve_setup = sem("dve_setup")
        row_loaded = sem("row_loaded")
        pT_loaded = sem("pT_loaded")
        w_loaded = [sem(f"w_loaded{i}") for i in range(W_SLOTS)]
        w_used = sem("w_used")
        consts_made = sem("consts_made")
        for_act = sem("bank_for_act")
        for_dve = sem("bank_for_dve")
        evacs = sem("evacs")
        act_ops = sem("act_ops")
        taken = sem("taken")
        dve_ops = sem("dve_ops")
        experts_ready = sem("experts_ready")
        staged_ready = sem("staged_ready")
        turn = sem("pool_turn")
        landed = [sem(f"landed{i}") for i in range(RING)]
        dve_rows = sem("dve_rows")
        pe_rows = sem("pe_rows")
        diag_ready = sem("diag_ready")
        gelu_ready = sem("gelu_ready")
        weight_ready = sem("weight_ready")
        sum_added = sem("sum_added")
        stored = sem("stored")

        def col(name, layer, i=0):
            j = COL_AT[name] + i
            return cols[:, layer, j:j + 1]

        block = ctx.enter_context(nc.Block())
        N_CONSTS = 6

        @block.sync
        def _(sp):
            sp.dma_start(ident[:, :], a["ident"]).then_inc(consts_loaded, 16)
            sp.dma_start(cols[:, :, :], a["cols"]).then_inc(consts_loaded, 16)
            for t in range(2):
                sp.dma_start(x[:, t, :], a["x"][t]).then_inc(x_loaded[t // 2], 16)
            sp.dma_start(lam_in, a["lam"]).then_inc(consts_loaded, 16)
            sp.dma_start(mla_rows[:, :, :, :], a["mla_rows"]).then_inc(consts_loaded, 16)
            sp.dma_start(rope_cos[:, :, :], a["rope"][0]).then_inc(consts_loaded, 16)
            sp.dma_start(rope_sin[:, :, :], a["rope"][1]).then_inc(consts_loaded, 16)
            sp.dma_start(ffn_row[:, :], a["ffn_rows"][0]).then_inc(row_loaded, 16)
            tile = 0

            def load(layer, first, widths):
                nonlocal tile
                for i, width in enumerate(widths):
                    if tile >= W_SLOTS:
                        name, count = TILE_DONE[tile - W_SLOTS]
                        sp.wait_ge({"w_used": w_used, "for_act": for_act, "for_dve": for_dve}[name], count)
                    sp.dma_start(wt[:, tile % W_SLOTS, 0:width], a["weights"][layer, first + i, :, 0:width])\
                        .then_inc(w_loaded[tile % W_SLOTS], 16)
                    tile += 1

            for step in range(-1, STEPS + 1):
                done, d = step - 1, step + 1
                if done >= 0:
                    if done >= 1:
                        sp.wait_ge(for_dve, WHERE[("ple_out", done - 1, 1)].taken + 2)
                    half = done % 2
                    sp.dma_start(pT[:, :, :], a["pT"][done // 2, :, :, half * HALF:(half + 1) * HALF])\
                        .then_inc(pT_loaded, 16)
                    load(done // 2, 0, PLE_TILES)
                if d == 0:
                    load(0, NT_PLE, DENSE_TILES[:4])
                    for t in range(2, 4):
                        sp.dma_start(x[:, t, :], a["x"][t]).then_inc(x_loaded[t // 2], 16)
                    load(0, NT_PLE + 4, DENSE_TILES[4:])
                elif d < STEPS:
                    if d == 2:
                        sp.wait_ge(dve_ops, WHERE[("ffn_norm", 1)].dve + 4)
                        sp.dma_start(ffn_row[:, :], a["ffn_rows"][1]).then_inc(row_loaded, 16)
                    load(d // 2, NT_PLE, DENSE_TILES)
                if done >= 2:
                    sp.wait_ge(dve_ops, WHERE[("ple_out", done, 1)].dve + 2)
                    for t in range(2):
                        sp.dma_start(a["out"][2 * (done % 2) + t], x[:, 2 * (done % 2) + t, :]).then_inc(stored, 16)
            sp.wait_ge(stored, 16 * 4)

        @block.gpsimd
        def _(pool):
            pool.iota(dist[:, :], [[1, 512]], base=-384, channel_multiplier=-1,
                      allow_small_or_imprecise_dtypes=True).then_inc(consts_made, 1)
            pool.memset(mask[:, :], 0.0).then_inc(consts_made, 1)
            pool.iota(iota[:, :], [[1, TOPK]], base=0, channel_multiplier=0,
                      allow_small_or_imprecise_dtypes=True).then_inc(consts_made, 1)
            pool.wait_ge(consts_made, 3)
            for m in (dist, mask):
                pool.affine_select(out=m[:, :], in_=m[:, :], compare_op=ALU.is_ge, fill=MASKED, base=384,
                                   pattern=[[-1, 512]], channel_multiplier=1).then_inc(consts_made, 1)
            n_staged = 0

            def group(step, phase, t, first, half, reg):
                table = a[f"{PHASES[phase].lower()}{step // 2}"]
                g = first if reg is None else first + 2 * reg
                columns = slice(g * RING, (g + 1) * RING) if reg is None else bass.ds(g * RING, RING)
                pool.tensor_copy(staged[:, half, :], experts[:, step % 2, t, columns]).then_inc(staged_ready, 1)
                pool.wait_ge(staged_ready, n_staged + 1 if reg is None else reg * 2 + (n_staged + 1))
                pool.sem_inc(turn, 1)
                before = (step, phase) if (first or reg is not None) else (step - (phase == 0), (phase - 1) % 4)
                for r in range(RING):
                    if before[0] >= 0:
                        by_dve = PHASES[before[1]] == "U" or r >= V_BY_PE
                        per = RING if PHASES[before[1]] == "U" else (V_BY_DVE if by_dve else V_BY_PE)
                        k = r if (PHASES[before[1]] == "U" or r < V_BY_PE) else r - V_BY_PE
                        rows_before = dve_rows_before(*before) if by_dve else pe_rows_before(*before)
                        count = rows_before + k + 1
                        if before == (step, phase):
                            count = count + (g - 1) * per
                        else:
                            count = count + (GROUPS - 1) * per
                        pool.wait_ge(dve_rows if by_dve else pe_rows, count)
                        pool.sem_inc(turn, 1)
                    pool.indirect_dma_start(
                        ring[:, r, :], None, table[:, :],
                        bass.IndirectOffsetOnAxis(ap=staged[:, half, r:r + 1], axis=0)).then_inc(landed[r], 16)

            for step in range(STEPS):
                for phase in range(4):
                    t = phase // 2
                    pool.wait_ge(experts_ready, 2 * step + t + 1)
                    group(step, phase, t, 0, 0, None)
                    n_staged += 1
                    with pool.Fori(0, GROUPS // 2 - 1) as i:
                        group(step, phase, t, 1, 1, i)
                        n_staged += 1
                        group(step, phase, t, 2, 0, i)
                        n_staged -= 1
                    n_staged += GROUPS - 2
                    group(step, phase, t, GROUPS - 1, 1, None)
                    n_staged += 1

        @block.scalar
        def _(act):
            n_bank = 0
            n_evac = 0
            n_op = 0

            def evac(out, in_, func=ACT.Copy, scale=1.0, last=True):
                nonlocal n_bank, n_evac, n_op
                act.wait_ge(for_act, n_bank + 1)
                ins = act.activation(out, in_, func, scale=scale)
                if last:
                    n_bank += 1
                    n_evac += 1
                    ins.then_inc(evacs, 1)
                else:
                    n_op += 1
                    ins.then_inc(act_ops, 1)

            def bank(width=512, sub=None):
                return ps_act[:, n_bank % 3, 0:width]

            def op(*args, **kw):
                nonlocal n_op
                act.activation(*args, **kw).then_inc(act_ops, 1)
                n_op += 1

            def square_sums(at, d):
                g0 = 2 * (d % 2)
                for t in range(2):
                    if t:
                        act.wait_ge(act_ops, n_op)
                    op(squares[:, 0:D], x[:, g0 + t, :], ACT.Square, accum_out=ss[:, t:t + 1])
                act.wait_ge(dve_ops, at.dve + 1)
                op(root[:, 0:2], mean_sq[:, 0:2], ACT.Sqrt)

            def norm(at, d, gain):
                act.wait_ge(dve_ops, at.dve)
                act.wait_ge(taken, at.taken)
                act.wait_ge(act_ops, at.act)
                act.wait_ge(evacs, at.evacs)
                square_sums(at, d)
                for k in range(KT):
                    evac(hT[:, k, :], bank(HALF), scale=1.0 if gain is None else col(gain, d // 2, k))

            def ple_norm(at, d):
                act.wait_ge(sum_added, 2 * d + 2)
                norm(at, d, "g_ple")

            def ple_out(at, d, n):
                for t in range(2):
                    act.wait_ge(taken, at.taken)
                    evac(gates[:, n, t, :], bank(), ACT.Sigmoid)

            def x_norm(at, d):
                if d < 2:
                    act.wait_ge(x_loaded[d], 16 * 2)
                norm(at, d, "g_mix")

            def qkv(at, d, n):
                for t in range(2):
                    out = diff_v[:, 2 * (d % 2) + t, :] if n == 2 else z[:, n, t, :]
                    evac(out, bank())

            def latents(at, d):
                for t in range(2):
                    evac(latent[:, t, :], bank(LATENT))

            def conv_c(at, d, i):
                act.wait_ge(act_ops, at.act)
                for c in range(2):
                    evac(conv_cT[:, 2 * i + c, :], bank(HALF))

            def conv_x(at, d, i):
                pass

            def conv_b(at, d, i):
                for c in range(2):
                    evac(conv_bT[:, 2 * i + c, :], bank(HALF))

            def taps(at, d):
                pass

            def diff_norm(at, d):
                act.wait_ge(dve_ops, at.dve + 3)
                op(root[:, 0:32], mean_sq[:, 0:32], ACT.Sqrt)

            def diff_turn(at, d):
                g0 = 2 * (d % 2)
                for h in range(DH):
                    evac(diff_qT[:, h, :], bank(HALF), scale=dq_gain[:, d // 2:d // 2 + 1])
                    evac(diff_kT[:, h, g0 * P:g0 * P + HALF], bank(HALF), scale=col("g_dk", d // 2))

            def width_of(d, t):
                return (2 * (d % 2) + t + 1) * P

            def diff_scores(at, d, t, h):
                b, w = h % 2, width_of(d, t)
                act.wait_ge(dve_ops, at.dve + 2)
                for m in range(2):
                    op(prob[:, b, m, 0:w], prob[:, b, m, 0:w], ACT.Exp, bias=neg_top[:, b, m:m + 1],
                       accum_out=total[:, b, m:m + 1])

            def diff_apply(at, d, t, h):
                w = width_of(d, t)
                evac(probT[:, h % 2, 0:w // P, :].rearrange("p k q -> p (k q)"), bank(w))
                evac(area_y[:, t, h * P:(h + 1) * P], bank(P))

            def diff_sub(at, d, t):
                act.wait_ge(dve_ops, at.dve + 3)
                op(root[:, 0:4], mean_sq[:, 0:4], ACT.Sqrt)
                evac(ydT[:, :, t * P:(t + 1) * P], bank().rearrange("p (k t) -> p k t", k=4),
                     scale=dsub_gain[:, d // 2:d // 2 + 1])

            def mla_norm(at, d):
                act.wait_ge(evacs, at.evacs)
                for t in range(2):
                    for i, (lo, hi) in enumerate(((0, QL), (QL, QL + KVL))):
                        op(area_e[:, (2 * t + i) * 256:(2 * t + i) * 256 + hi - lo], latent[:, t, lo:hi], ACT.Square,
                           accum_out=ss[:, 2 * i + t:2 * i + t + 1])
                act.wait_ge(dve_ops, at.dve + 2)
                op(root[:, 0:4], mean_sq[:, 0:4], ACT.Sqrt)
                for k in range(2):
                    evac(cqT[:, k, :], bank(HALF), scale=col("g_cq", d // 2, k))
                evac(ckvT, bank(HALF), scale=col("g_ckv", d // 2))

            def mla_up(at, d):
                for t in range(2):
                    row = qm[:, t, :, :].rearrange("p h d -> p (h d)")
                    evac(row[:, 0:512], bank())
                    evac(row[:, 512:768], bank(256))
                    for i in range(2):
                        part = bank().rearrange("p (h d) -> p h d", h=4)
                        evac(km[:, t, 4 * i:4 * i + 4, 0:MNOPE], part[:, :, 0:MNOPE], last=False)
                        evac(mla_v[:, 2 * (d % 2) + t, 256 * i:256 * (i + 1)].rearrange("p (h d) -> p h d", h=4),
                             part[:, :, MNOPE:MNOPE + MV])

            def mla_qk(at, d):
                act.wait_ge(dve_ops, at.dve + 8)
                op(root[:, 0:32], mean_sq[:, 0:32], ACT.Sqrt)

            def mla_turn(at, d):
                g0 = 2 * (d % 2)
                for h in range(MH):
                    evac(mla_qT[0:MQK, h, :], bank(HALF)[0:MQK], scale=float(MQK) ** -0.5)
                    evac(mla_kT[0:MQK, h, g0 * P:g0 * P + HALF], bank(HALF)[0:MQK])

            def mla_scores(at, d, t, h):
                b, w = h % 2, width_of(d, t)
                act.wait_ge(dve_ops, at.dve + 1)
                op(prob[:, b, 0, 0:w], prob[:, b, 0, 0:w], ACT.Exp, bias=neg_top[:, b, 0:1],
                   accum_out=total[:, b, 0:1])

            def mla_apply(at, d, t, h):
                w = width_of(d, t)
                evac(probT[:, h % 2, 0:w // P, :].rearrange("p k q -> p (k q)"), bank(w))
                act.wait_ge(dve_ops, at.dve + 1)
                evac(area_y[:, t, h * MV:(h + 1) * MV], bank(MV), scale=inv[:, h % 2, 0:1])

            def mla_out(at, d, t):
                evac(ymT[:, :, t * P:(t + 1) * P], bank().rearrange("p (k t) -> p k t", k=4))

            def mix(at, d, n, br):
                for t in range(2):
                    act.wait_ge(taken, at.taken - (2 if br or n else 0))
                    if not (br or n):
                        act.wait_ge(act_ops, at.act)
                    evac(gates[:, (3 * n + br) % 2, t, :], bank(), ACT.Sigmoid)

            def mix_turn(at, d):
                for k in range(KT):
                    evac(mixedT[:, k, :], bank(HALF))

            def out(at, d, n):
                pass

            def ffn_norm(at, d):
                norm(at, d, None)

            def query(at, d, i):
                for c in range(2):
                    evac(queryT[:, 2 * i + c, :], bank(HALF))

            def scores(at, d, t):
                act.wait_ge(dve_ops, at.dve)
                act.wait_ge(act_ops, at.act)
                for i in range(4):
                    evac(key_scores[:, 4 * i:4 * i + 4, :].rearrange("p c n -> p (c n)"), bank())

            def topk(at, d, t):
                act.wait_ge(dve_ops, at.dve + 132)
                op(exps, exps, ACT.Exp)

            stage = dict(ple_norm=ple_norm, ple_out=ple_out, x_norm=x_norm, qkv=qkv, latent=latents, conv_c=conv_c,
                         conv_x=conv_x, conv_b=conv_b, taps=taps, diff_norm=diff_norm, diff_turn=diff_turn,
                         diff_scores=diff_scores, diff_apply=diff_apply, diff_sub=diff_sub, mla_norm=mla_norm,
                         mla_up=mla_up, mla_qk=mla_qk, mla_turn=mla_turn, mla_scores=mla_scores,
                         mla_apply=mla_apply, mla_out=mla_out, mix_first=mix, mix_more=mix, mix_turn=mix_turn,
                         out=out, ffn_norm=ffn_norm, query=query, scores=scores, topk=topk)
            rows = Rows()

            def make_diag(step, phase, g):
                for r in range(V_BY_PE):
                    j = g * RING + r
                    if isinstance(g, int) and g == 0:
                        if pe_rows_before(step, phase):
                            act.wait_ge(pe_rows, pe_rows_before(step, phase) - V_BY_PE + r + 1)
                    else:
                        act.wait_ge(pe_rows, (g - 1) * V_BY_PE + (pe_rows_before(step, phase) + r + 1))
                    column = weight[:, j:j + 1] if isinstance(g, int) else weight[:, bass.ds(j, 1)]
                    act.activation(diag[:, r, :], ident[:, :], ACT.Copy, scale=column).then_inc(diag_ready, 1)

            def serve(n):
                for phase, first, m in rows.parts(n):
                    step = rows.step
                    if PHASES[phase] == "U":
                        if first + m == GROUPS:
                            act.wait_ge(dve_rows, dve_rows_before(step, phase) + ROWS)
                            act.activation(dots[:, :], dots[:, :], ACT.Gelu).then_inc(gelu_ready, 1)
                        continue
                    if first == 0:
                        act.wait_ge(weight_ready, 2 * step + phase // 2 + 1)
                        make_diag(step, phase, 0)
                        first, m = 1, m - 1
                    if m > 1:
                        with act.Fori(0, m) as i:
                            make_diag(step, phase, i + first)
                    elif m:
                        make_diag(step, phase, first)

            act.wait_ge(consts_loaded, 16 * N_CONSTS)
            act.wait_ge(consts_made, 5 + 1)
            act.activation(lam[:, :, 0:2], lam[:, :, 0:2], ACT.Exp).then_inc(consts_made, 1)
            for step, row, rest in PLAN:
                rows.step, rows.pos = step, 0
                for (name, d, *more), at, groups in row:
                    assert (n_evac, n_op) == (at.evacs, at.act), (name, d, more, n_evac, n_op, at.evacs, at.act)
                    stage[name](at, d, *more)
                    serve(groups)
                serve(rest)

        @block.vector
        def _(dve):
            n_bank = 0
            n_op = 0

            def op(ins):
                nonlocal n_op
                ins.then_inc(dve_ops, 1)
                n_op += 1

            def take(ins):
                nonlocal n_bank
                ins.then_inc(taken, 1)
                n_bank += 1

            def bank(width=512):
                dve.wait_ge(for_dve, n_bank + 1)
                return ps_dve[:, n_bank % 3, 0:width]

            def link():
                dve.wait_ge(dve_ops, n_op)

            def mean(out, in_, n):
                op(dve.tensor_scalar(out, in_, 1.0 / n, EPS, ALU.mult, ALU.add))

            def norm(at, d, ffn):
                g0 = 2 * (d % 2)
                dve.wait_ge(taken, n_bank)
                link()
                dve.wait_ge(act_ops, at.act + 2)
                mean(mean_sq[:, 0:2], ss[:, 0:2], D)
                dve.wait_ge(act_ops, at.act + 3)
                link()
                op(dve.reciprocal(rstd[:, 0:2], root[:, 0:2]))
                link()
                if ffn:
                    dve.wait_ge(row_loaded, 16 * (d // 2 + 1))
                    if d:
                        dve.wait_ge(dve_rows, dve_rows_before(d - 1, 2) + ROWS)
                for t in range(2):
                    if ffn:
                        op(dve.scalar_tensor_tensor(h_ffn[:, t, :], x[:, g0 + t, :], rstd[:, t:t + 1], ffn_row[:, :],
                                                    ALU.mult, ALU.mult))
                    else:
                        op(dve.tensor_scalar(normed[:, t, :], x[:, g0 + t, :], rstd[:, t:t + 1], None, ALU.mult))

            def ple_norm(at, d):
                dve.wait_ge(sum_added, 2 * d + 2)
                norm(at, d, False)

            def ple_out(at, d, n):
                g0 = 2 * (d % 2)
                link()
                for t in range(2):
                    dve.wait_ge(evacs, at.evacs + t + 1)
                    take(dve.tensor_tensor(product[:, t, :], bank(), gates[:, n, t, :], ALU.mult))
                dve.wait_ge(taken, n_bank)
                for t in range(2):
                    xs = x[:, g0 + t, n * 512:(n + 1) * 512]
                    op(dve.tensor_tensor(xs, xs, product[:, t, :], ALU.add))

            def x_norm(at, d):
                norm(at, d, False)

            def nothing(at, d, *more):
                pass

            def conv_x(at, d, i):
                dve.wait_ge(evacs, WHERE[("conv_c", d, 1)].evacs + 2)
                for c in range(2):
                    take(dve.tensor_tensor(conv_u[:, 2 * i + c, 2:2 + HALF], bank(HALF), conv_cT[:, 2 * i + c, :],
                                           ALU.mult))

            def taps(at, d):
                if d % 2:
                    op(dve.tensor_copy(conv_u[:, :, 0:2], tail[:, :, :]))
                else:
                    op(dve.memset(conv_u[:, :, 0:2], 0.0))
                link()
                dve.wait_ge(taken, n_bank)
                for j in range(3):
                    for c in range(4):
                        u = conv_u[:, c, j:j + HALF]
                        if j == 0:
                            op(dve.tensor_scalar(ycT[:, c, :], u, col("conv", d // 2, c), None, ALU.mult))
                        else:
                            op(dve.scalar_tensor_tensor(ycT[:, c, :], u, col("conv", d // 2, 4 * j + c), ycT[:, c, :],
                                                        ALU.mult, ALU.add))
                    link()
                dve.wait_ge(evacs, at.evacs)
                op(dve.tensor_tensor(ycT, ycT, conv_bT, ALU.mult))
                op(dve.tensor_copy(tail[:, :, :], conv_u[:, :, HALF:HALF + 2]))

            def diff_norm(at, d):
                link()
                dve.wait_ge(evacs, at.evacs)
                flat = area_b[:, 0:2048]
                op(dve.tensor_tensor(squares, flat, flat, ALU.mult))
                link()
                op(dve.tensor_reduce(ss, squares.rearrange("p (g d) -> p g d", d=DHD), AX, ALU.add))
                link()
                mean(mean_sq, ss, DHD)
                dve.wait_ge(act_ops, at.act + 1)
                op(dve.reciprocal(rstd[:, :], root))
                link()
                groups = flat.rearrange("p (g d) -> p g d", d=DHD)
                op(dve.tensor_tensor(groups, groups, rstd[:, :].unsqueeze(2).to_broadcast([P, 32, DHD]), ALU.mult))

            def window(m, d, t):
                g = 2 * (d % 2) + t
                return m[:, 384 - g * P:512]

            def diff_scores(at, d, t, h):
                b, w = h % 2, (2 * (d % 2) + t + 1) * P
                dve.wait_ge(evacs, at.evacs)
                link()
                for m in range(2):
                    take(dve.scalar_tensor_tensor(prob[:, b, m, 0:w], window(dist, d, t), SLOPES[h], bank(w),
                                                  ALU.mult, ALU.add))
                dve.wait_ge(taken, n_bank)
                for m in range(2):
                    op(dve.tensor_reduce(neg_top[:, b, m:m + 1], prob[:, b, m, 0:w], AX, ALU.max, negate=True))

            def diff_apply(at, d, t, h):
                b, w = h % 2, (2 * (d % 2) + t + 1) * P
                dve.wait_ge(act_ops, WHERE[("diff_scores", d, t, h)].act + 2)
                op(dve.reciprocal(inv[:, b, :], total[:, b, :]))
                link()
                op(dve.tensor_scalar(inv_lam[:, b:b + 1], inv[:, b, 1:2], lam[:, d // 2, 3:4], None, ALU.mult))
                op(dve.tensor_scalar(prob[:, b, 0, 0:w], prob[:, b, 0, 0:w], inv[:, b, 0:1], None, ALU.mult))
                link()
                op(dve.scalar_tensor_tensor(prob[:, b, 0, 0:w], prob[:, b, 1, 0:w], inv_lam[:, b:b + 1],
                                            prob[:, b, 0, 0:w], ALU.mult, ALU.add))

            def diff_sub(at, d, t):
                y = area_y[:, t, :]
                dve.wait_ge(evacs, at.evacs)
                link()
                op(dve.tensor_tensor(scratch[:, :], y, y, ALU.mult))
                link()
                op(dve.tensor_reduce(ss[:, 0:4], scratch[:, :].rearrange("p (g d) -> p g d", d=P), AX, ALU.add))
                link()
                mean(mean_sq[:, 0:4], ss[:, 0:4], P)
                dve.wait_ge(act_ops, at.act + 1)
                op(dve.reciprocal(rstd[:, 0:4], root[:, 0:4]))
                link()
                heads = y.rearrange("p (h d) -> p h d", h=DH)
                op(dve.tensor_tensor(heads, heads, rstd[:, 0:4].unsqueeze(2).to_broadcast([P, DH, P]), ALU.mult))

            def mla_norm(at, d):
                dve.wait_ge(act_ops, at.act + 4)
                mean(mean_sq[:, 0:2], ss[:, 0:2], QL)
                mean(mean_sq[:, 2:4], ss[:, 2:4], KVL)
                dve.wait_ge(act_ops, at.act + 5)
                op(dve.reciprocal(rstd[:, 0:4], root[:, 0:4]))
                link()
                for i, (lo, hi) in enumerate(((0, QL), (QL, QL + KVL))):
                    part = latent[:, :, lo:hi]
                    r = rstd[:, 2 * i:2 * i + 2].unsqueeze(2).to_broadcast([P, 2, hi - lo])
                    op(dve.tensor_tensor(part, part, r, ALU.mult))

            def mla_qk(at, d):
                layer, g0 = d // 2, 2 * (d % 2)
                kr = latent[:, :, QL + KVL:LATENT]
                q16 = area_b[:, 0:1536].rearrange("p (g d) -> p g d", d=MQK)
                k16 = area_b[:, 1536:3072].rearrange("p (g d) -> p g d", d=MQK)[:, :, 0:MNOPE]
                gq, gk = mla_rows[:, layer, 0, :], mla_rows[:, layer, 1, :]
                sq = area_e[:, 0:1536].rearrange("p (g d) -> p g d", d=MQK)
                sk = area_e[:, 0:1024].rearrange("p (g d) -> p g d", d=MNOPE)
                dve.wait_ge(evacs, at.evacs)
                dve.wait_ge(act_ops, at.act)
                link()
                op(dve.tensor_tensor(sq, q16, q16, ALU.mult))
                link()
                op(dve.tensor_reduce(ss[:, 0:16], sq, AX, ALU.add))
                link()
                op(dve.tensor_tensor(sk, k16, k16, ALU.mult))
                link()
                op(dve.tensor_reduce(ss[:, 16:32], sk, AX, ALU.add))
                kr2 = scratch[:, 0:64].rearrange("p (t d) -> p t d", t=2)
                op(dve.tensor_tensor(kr2, kr, kr, ALU.mult))
                link()
                op(dve.tensor_reduce(ss_rope, kr2, AX, ALU.add))
                link()
                kss = ss[:, 16:32].rearrange("p (t h) -> p t h", t=2)
                op(dve.tensor_tensor(kss, kss, ss_rope.unsqueeze(2).to_broadcast([P, 2, MH]), ALU.add))
                link()
                mean(mean_sq, ss, MQK)
                dve.wait_ge(act_ops, at.act + 1)
                op(dve.reciprocal(rstd[:, :], root))
                link()
                op(dve.tensor_tensor(q16, q16, rstd[:, 0:16].unsqueeze(2).to_broadcast([P, 16, MQK]), ALU.mult))
                op(dve.tensor_tensor(k16, k16, rstd[:, 16:32].unsqueeze(2).to_broadcast([P, 16, MNOPE]), ALU.mult))
                link()
                op(dve.tensor_tensor(q16, q16, gq.unsqueeze(1).to_broadcast([P, 16, MQK]), ALU.mult))
                op(dve.tensor_tensor(k16, k16, gk[:, 0:MNOPE].unsqueeze(1).to_broadcast([P, 16, MNOPE]), ALU.mult))
                op(dve.tensor_tensor(kr, kr, gk[:, MNOPE:MQK].unsqueeze(1).to_broadcast([P, 2, MROPE]), ALU.mult))
                link()
                krs = scratch[:, 64:128].rearrange("p (t d) -> p t d", t=2)
                cos, sin = rope_cos[:, g0:g0 + 2, :], rope_sin[:, g0:g0 + 2, :]
                hr = MROPE // 2
                op(dve.tensor_tensor(krs[:, :, 0:hr], kr[:, :, hr:MROPE], sin[:, :, 0:hr], ALU.mult))
                op(dve.tensor_tensor(krs[:, :, hr:MROPE], kr[:, :, 0:hr], sin[:, :, hr:MROPE], ALU.mult))
                link()
                op(dve.tensor_tensor(kr, kr, cos, ALU.mult))
                link()
                op(dve.tensor_tensor(kr, kr, krs, ALU.add))
                link()
                for t in range(2):
                    r = rstd[:, 16 + MH * t:16 + MH * (t + 1)].unsqueeze(2).to_broadcast([P, MH, MROPE])
                    op(dve.tensor_tensor(km[:, t, :, MNOPE:MQK], kr[:, t, :].unsqueeze(1).to_broadcast([P, MH, MROPE]),
                                         r, ALU.mult))
                turned = scratch[:, :].rearrange("p (t h d) -> p t h d", t=2, h=MH)
                for t in range(2):
                    xr = qm[:, t, :, MNOPE:MQK]
                    s = rope_sin[:, g0 + t, :].unsqueeze(1).to_broadcast([P, MH, MROPE])
                    op(dve.tensor_tensor(turned[:, t, :, 0:hr], xr[:, :, hr:MROPE], s[:, :, 0:hr], ALU.mult))
                    op(dve.tensor_tensor(turned[:, t, :, hr:MROPE], xr[:, :, 0:hr], s[:, :, hr:MROPE], ALU.mult))
                link()
                for t in range(2):
                    xr = qm[:, t, :, MNOPE:MQK]
                    c = rope_cos[:, g0 + t, :].unsqueeze(1).to_broadcast([P, MH, MROPE])
                    op(dve.tensor_tensor(xr, xr, c, ALU.mult))
                link()
                for t in range(2):
                    xr = qm[:, t, :, MNOPE:MQK]
                    op(dve.tensor_tensor(xr, xr, turned[:, t, :, :], ALU.add))

            def mla_scores(at, d, t, h):
                b, w = h % 2, (2 * (d % 2) + t + 1) * P
                dve.wait_ge(evacs, at.evacs)
                take(dve.tensor_tensor_reduce(prob[:, b, 0, 0:w], bank(w), window(mask, d, t), 1.0, LOWEST,
                                              ALU.add, ALU.max, top[:, b, 0:1]))
                dve.wait_ge(taken, n_bank)
                op(dve.tensor_scalar(neg_top[:, b, 0:1], top[:, b, 0:1], -1.0, None, ALU.mult))

            def mla_apply(at, d, t, h):
                b = h % 2
                dve.wait_ge(act_ops, WHERE[("mla_scores", d, t, h)].act + 1)
                op(dve.reciprocal(inv[:, b, 0:1], total[:, b, 0:1]))

            def mix(at, d, n, br):
                for t in range(2):
                    dve.wait_ge(evacs, at.evacs + t + 1)
                    s = gates[:, (3 * n + br) % 2, t, :]
                    if br == 0:
                        take(dve.tensor_tensor(mixed[:, t, n * 512:(n + 1) * 512], bank(), s, ALU.mult))
                    else:
                        if t == 0:
                            link()
                        take(dve.tensor_tensor(product[:, t, :], bank(), s, ALU.mult))
                if br:
                    dve.wait_ge(taken, n_bank)
                    for t in range(2):
                        m = mixed[:, t, n * 512:(n + 1) * 512]
                        op(dve.tensor_tensor(m, m, product[:, t, :], ALU.add))

            def out(at, d, n):
                for t in range(2):
                    xs = x[:, 2 * (d % 2) + t, n * 512:(n + 1) * 512]
                    take(dve.tensor_tensor(xs, bank(), xs, ALU.add))

            def ffn_norm(at, d):
                norm(at, d, True)

            def topk(at, d, t):
                start = n_op
                dve.wait_ge(evacs, at.evacs)
                link()
                for c in range(HP):
                    op(dve.max(top_v[:, c, 0:8], key_scores[:, c, :]))
                link()
                for c in range(HP):
                    op(dve.max_index(top_i[:, c, 0:8], top_v[:, c, 0:8], key_scores[:, c, :]))
                link()
                for c in range(HP):
                    op(dve.match_replace(key_scores[:, c, :], top_v[:, c, 0:8], key_scores[:, c, :], LOWEST))
                link()
                for c in range(HP):
                    op(dve.max(top_v[:, c, 8:16], key_scores[:, c, :]))
                link()
                for c in range(HP):
                    op(dve.max_index(top_i[:, c, 8:16], top_v[:, c, 8:16], key_scores[:, c, :]))
                sums = cand.rearrange("p (h i j) -> p h i j", h=HEADS, i=TOPK)
                pair = top_v.rearrange("p (h c) k -> p h c k", c=2)
                shape = [P, HEADS, TOPK, TOPK]
                op(dve.tensor_tensor(sums, pair[:, :, 0, :].unsqueeze(3).to_broadcast(shape),
                                     pair[:, :, 1, :].unsqueeze(2).to_broadcast(shape), ALU.add))
                link()
                op(dve.tensor_copy(top_f.rearrange("p h c k -> p (h c k)"), top_i.rearrange("p c k -> p (c k)")))
                lists = cand.rearrange("p (h c) -> p h c", h=HEADS)
                for h in range(HEADS):
                    op(dve.max(best_v[:, h, 0:8], lists[:, h, :]))
                link()
                for h in range(HEADS):
                    op(dve.max_index(best_c[:, h, 0:8], best_v[:, h, 0:8], lists[:, h, :]))
                link()
                for h in range(HEADS):
                    op(dve.match_replace(lists[:, h, :], best_v[:, h, 0:8], lists[:, h, :], LOWEST))
                link()
                for h in range(HEADS):
                    op(dve.max(best_v[:, h, 8:16], lists[:, h, :]))
                link()
                for h in range(HEADS):
                    op(dve.max_index(best_c[:, h, 8:16], best_v[:, h, 8:16], lists[:, h, :]))
                link()
                places = best_c.rearrange("p h k -> p (h k)")
                op(dve.tensor_scalar(part_u[:, 0, :], places, 4, None, ALU.logical_shift_right))
                op(dve.tensor_scalar(part_u[:, 1, :], places, 15, None, ALU.bitwise_and))
                link()
                op(dve.tensor_copy(part_f.rearrange("p c h k -> p (c h k)"), part_u.rearrange("p c k -> p (c k)")))
                link()
                for c in range(2):
                    op(dve.tensor_tensor(sums, part_f[:, c, :, :].unsqueeze(3).to_broadcast(shape),
                                         iota[:, :].unsqueeze(1).unsqueeze(1).to_broadcast(shape), ALU.is_equal))
                    link()
                    op(dve.tensor_tensor(sums, sums, top_f[:, :, c, :].unsqueeze(2).to_broadcast(shape), ALU.mult))
                    link()
                    op(dve.tensor_reduce(part_i[:, c, :], cand.rearrange("p (g i) -> p g i", i=TOPK), AX, ALU.add))
                    link()
                dve.scalar_tensor_tensor(experts[:, d % 2, t, :], part_i[:, 0, :], 128.0, part_i[:, 1, :],
                                         ALU.mult, ALU.add).then_inc(experts_ready, 1)
                op(dve.tensor_tensor(exps, best_v, best_v[:, :, 0:1].to_broadcast([P, HEADS, TOPK]), ALU.subtract))
                assert n_op - start == 132, n_op - start
                dve.wait_ge(act_ops, at.act + 1)
                op(dve.tensor_reduce(esum, exps, AX, ALU.add))
                link()
                op(dve.reciprocal(esum, esum))
                link()
                op(dve.tensor_tensor(gate[:, d % 2, t, :].rearrange("p (h k) -> p h k", h=HEADS), exps,
                                     esum.unsqueeze(2).to_broadcast([P, HEADS, TOPK]), ALU.mult))

            stage = dict(ple_norm=ple_norm, ple_out=ple_out, x_norm=x_norm, qkv=nothing, latent=nothing,
                         conv_c=nothing, conv_x=conv_x, conv_b=nothing, taps=taps, diff_norm=diff_norm,
                         diff_turn=nothing, diff_scores=diff_scores, diff_apply=diff_apply, diff_sub=diff_sub,
                         mla_norm=mla_norm, mla_up=nothing, mla_qk=mla_qk, mla_turn=nothing,
                         mla_scores=mla_scores, mla_apply=mla_apply, mla_out=nothing, mix_first=mix, mix_more=mix,
                         mix_turn=nothing, out=out, ffn_norm=ffn_norm, query=nothing, scores=nothing, topk=topk)
            rows = Rows()

            def group(step, phase, t, g):
                filled = turns_before(step, phase)
                for r in range(RING) if PHASES[phase] == "U" else range(V_BY_PE, RING):
                    j = g * RING + r
                    column = slice(j, j + 1) if isinstance(g, int) else bass.ds(j, 1)
                    dve.wait_ge(landed[r], (g + (filled + 1)) * 16)
                    if PHASES[phase] == "U":
                        dve.scalar_tensor_tensor(ring[:, r, :], ring[:, r, :], 1.0, h_ffn[:, t, :], ALU.mult, ALU.mult,
                                                 accum_out=dots[:, column]).then_inc(dve_rows, 1)
                    else:
                        before = dve_rows_before(step, phase) + r - V_BY_PE
                        dve.wait_ge(dve_rows, g * V_BY_DVE + before)
                        xs = x[:, 2 * (step % 2) + t, :]
                        dve.scalar_tensor_tensor(xs, ring[:, r, :], weight[:, column], xs, ALU.mult, ALU.add)\
                            .then_inc(dve_rows, 1)

            def serve(n):
                for phase, first, m in rows.parts(n):
                    step, t = rows.step, phase // 2
                    if first == 0:
                        link()
                        dve.wait_ge(taken, n_bank)
                        if PHASES[phase] == "V":
                            dve.wait_ge(weight_ready, 2 * step + t + 1)
                    if m > 1:
                        with dve.Fori(0, m) as i:
                            group(step, phase, t, i + first)
                    else:
                        group(step, phase, t, first)
                    if first + m < GROUPS:
                        continue
                    if PHASES[phase] == "U":
                        dve.wait_ge(gelu_ready, 2 * step + t + 1)
                        dve.tensor_tensor(weight[:, :], gate[:, step % 2, t, :], dots[:, :], ALU.mult)\
                            .then_inc(weight_ready, 1)
                    else:
                        dve.wait_ge(pe_rows, pe_rows_before(step, phase) + GROUPS * V_BY_PE)
                        dve.wait_ge(dve_rows, dve_rows_before(step, phase) + GROUPS * V_BY_DVE)
                        xs = x[:, 2 * (step % 2) + t, :]
                        dve.tensor_tensor(xs, ps_sum[:, :, :].rearrange("p b n -> p (b n)"), xs, ALU.add)\
                            .then_inc(sum_added, 1)

            dve.wait_ge(consts_loaded, 16 * N_CONSTS)
            dve.wait_ge(consts_made, 5)
            products = scratch[:, 0:4 * DHD].rearrange("p (l c d) -> p l c d", l=DEPTH, c=2)
            n_setup = 0

            def make(ins):
                nonlocal n_setup
                ins.then_inc(dve_setup, 1)
                n_setup += 1
                dve.wait_ge(dve_setup, n_setup)
            pairs = lam_in.rearrange("p l (c two) d -> p l c two d", two=2)
            for layer in range(DEPTH):
                make(dve.tensor_tensor(products[:, layer, :, :], pairs[:, layer, :, 0, :], pairs[:, layer, :, 1, :], ALU.mult))
            for layer in range(DEPTH):
                make(dve.tensor_reduce(lam[:, layer, 0:2], products[:, layer, :, :], AX, ALU.add))
                make(dve.tensor_scalar(dq_gain[:, layer:layer + 1], col("g_dq", layer), float(DHD) ** -0.5, None, ALU.mult))
                make(dve.tensor_scalar(dsub_gain[:, layer:layer + 1], col("g_dsub", layer), 1.0 - LAMBDA_INIT[layer],
                                       None, ALU.mult))
            dve.memset(scratch[:, 0:1], 0.0).then_inc(consts_made, 1)
            dve.wait_ge(consts_made, 7)
            for layer in range(DEPTH):
                make(dve.tensor_tensor(lam[:, layer, 2:3], lam[:, layer, 1:2], lam[:, layer, 0:1], ALU.subtract))
                make(dve.tensor_scalar(lam[:, layer, 3:4], lam[:, layer, 2:3], LAMBDA_INIT[layer], None, ALU.subtract))
            for step, row, rest in PLAN:
                rows.step, rows.pos = step, 0
                for (name, d, *more), at, groups in row:
                    assert (n_bank, n_op) == (at.taken, at.dve), (name, d, more, n_bank, n_op, at.taken, at.dve)
                    stage[name](at, d, *more)
                    serve(groups)
                serve(rest)

        @block.tensor
        def _(pe):
            n_act = 0
            n_dve = 0
            n_tile = 0

            def act_bank(k=0):
                if n_act + k >= 3:
                    pe.wait_ge(evacs, n_act + k - 2)
                return ps_act[:, (n_act + k) % 3, :]

            def dve_bank(k=0):
                if n_dve + k >= 3:
                    pe.wait_ge(taken, n_dve + k - 2)
                return ps_dve[:, (n_dve + k) % 3, :]

            def to_act(ins):
                nonlocal n_act
                ins.then_inc(for_act, 1)
                n_act += 1

            def to_dve(ins):
                nonlocal n_dve
                ins.then_inc(for_dve, 1)
                n_dve += 1

            def tile(k=0):
                slot, use = (n_tile + k) % W_SLOTS, (n_tile + k) // W_SLOTS
                pe.wait_ge(w_loaded[slot], 16 * (use + 1))
                return wt[:, slot, :]

            def release(n):
                nonlocal n_tile
                n_tile += n

            def turn_tiles(source, wait=None):
                b = act_bank()
                for t in range(2):
                    s = source(t)
                    ins = pe.transpose(b[0:s.shape[1], t * P:(t + 1) * P], s, ident[:, :])
                to_act(ins)

            def norm(at, d, source):
                pe.wait_ge(dve_ops, at.dve + 4)
                for k in range(KT):
                    turn_tiles(lambda t: source[:, t, k * P:(k + 1) * P])

            def rows_by_columns(lhsT, banks, width=512):
                last = []
                for kh in range(2):
                    w = tile(kh).rearrange("p (k n) -> p k n", k=4)
                    for t in range(2):
                        for k in range(4):
                            ins = pe.matmul(banks[t][:, 0:width], lhsT[:, 4 * kh + k, t * P:(t + 1) * P],
                                            w[:, k, 0:width], start=(kh + k == 0), stop=(kh == 1 and k == 3))
                        last.append(ins)
                last[1].then_inc(w_used, 1)
                return last[2:]

            def hT_ready(at):
                pe.wait_ge(evacs, at.evacs)

            def ple_norm(at, d):
                norm(at, d, normed)

            def ple_out(at, d, n):
                hT_ready(WHERE[("ple_out", d, 0)])
                for ins in rows_by_columns(hT, [act_bank(0), act_bank(1)]):
                    to_act(ins)
                pe.wait_ge(pT_loaded, 16 * (d + 1))
                w = tile(2).rearrange("p (k n) -> p k n", k=4)
                for t in range(2):
                    b = dve_bank()
                    for k in range(2):
                        ins = pe.matmul(b, pT[:, k, t * P:(t + 1) * P], w[:, k, :], start=(k == 0), stop=(k == 1))
                    to_dve(ins)
                release(3)

            def x_norm(at, d):
                norm(at, d, normed)

            def qkv(at, d, n):
                hT_ready(WHERE[("qkv", d, 0)])
                for ins in rows_by_columns(hT, [act_bank(0), act_bank(1)]):
                    to_act(ins)
                release(2)

            def latents(at, d):
                for ins in rows_by_columns(hT, [act_bank(0), act_bank(1)], LATENT):
                    to_act(ins)
                release(2)

            def columns_by_tokens(to, get_bank):
                w = tile().rearrange("p (k n) -> p k n", k=KT)
                for c in range(2):
                    b = get_bank()
                    for k in range(KT):
                        ins = pe.matmul(b[:, 0:HALF], w[:, k, c * P:(c + 1) * P], hT[:, k, :],
                                        start=(k == 0), stop=(k == KT - 1))
                    to(ins)
                release(1)

            def conv(at, d, i):
                columns_by_tokens(to_act, act_bank)

            def conv_x(at, d, i):
                columns_by_tokens(to_dve, dve_bank)

            def nothing(at, d, *more):
                pass

            def diff_turn(at, d):
                pe.wait_ge(dve_ops, at.dve)
                for h in range(DH):
                    for c in range(2):
                        turn_tiles(lambda t: z[:, c, t, h * P:(h + 1) * P])

            def diff_scores(at, d, t, h):
                w = (2 * (d % 2) + t + 1) * P
                pe.wait_ge(evacs, WHERE[("diff_turn", d)].evacs + 8)
                for m in range(2):
                    b = dve_bank()
                    lo, hi = m * DHD, (m + 1) * DHD
                    to_dve(pe.matmul(b[:, 0:w], diff_qT[lo:hi, h, t * P:(t + 1) * P], diff_kT[lo:hi, h, 0:w],
                                     start=True, stop=True))

            def apply(t, h, d, v, dv, first):
                b, blocks = h % 2, 2 * (d % 2) + t + 1
                bank = act_bank()
                for k in range(blocks):
                    ins = pe.transpose(bank[:, k * P:(k + 1) * P], prob[:, b, 0, k * P:(k + 1) * P], ident[:, :])
                to_act(ins)
                bank = act_bank()
                pe.wait_ge(evacs, first + 1)
                for k in range(blocks):
                    ins = pe.matmul(bank[:, 0:dv], probT[:, b, k, :], v[:, k, h * dv:(h + 1) * dv],
                                    start=(k == 0), stop=(k == blocks - 1))
                to_act(ins)

            def diff_apply(at, d, t, h):
                pe.wait_ge(dve_ops, at.dve + 4)
                apply(t, h, d, diff_v, P, at.evacs)

            def turn_rows(t):
                bank = act_bank()
                for k in range(4):
                    ins = pe.transpose(bank[:, k * P:(k + 1) * P], area_y[:, t, k * P:(k + 1) * P], ident[:, :])
                to_act(ins)

            def diff_sub(at, d, t):
                pe.wait_ge(dve_ops, at.dve + 5)
                turn_rows(t)

            def mla_norm(at, d):
                pe.wait_ge(dve_ops, at.dve + 5)
                for k in range(3):
                    turn_tiles(lambda t: latent[:, t, k * P:(k + 1) * P])

            def mla_up(at, d):
                pe.wait_ge(evacs, at.evacs)
                uq = tile(0)[:, 0:1536].rearrange("p (k n) -> p k n", k=2)
                ukv = tile(1)
                for t in range(2):
                    ts = slice(t * P, (t + 1) * P)
                    for lo, hi in ((0, 512), (512, 768)):
                        b = act_bank()
                        for k in range(2):
                            ins = pe.matmul(b[:, 0:hi - lo], cqT[:, k, ts], uq[:, k, lo:hi], start=(k == 0), stop=(k == 1))
                        to_act(ins)
                    for i in range(2):
                        to_act(pe.matmul(act_bank(), ckvT[:, ts], ukv[:, 512 * i:512 * (i + 1)], start=True, stop=True))
                release(2)

            def mla_turn(at, d):
                pe.wait_ge(dve_ops, at.dve)
                for h in range(MH):
                    for source in (qm, km):
                        turn_tiles(lambda t: source[:, t, h, :])

            def mla_scores(at, d, t, h):
                w = (2 * (d % 2) + t + 1) * P
                pe.wait_ge(evacs, WHERE[("mla_turn", d)].evacs + 16)
                b = dve_bank()
                to_dve(pe.matmul(b[:, 0:w], mla_qT[0:MQK, h, t * P:(t + 1) * P], mla_kT[0:MQK, h, 0:w],
                                 start=True, stop=True))

            def mla_apply(at, d, t, h):
                pe.wait_ge(act_ops, WHERE[("mla_scores", d, t, h)].act + 1)
                apply(t, h, d, mla_v, MV, at.evacs)

            def mla_out(at, d, t):
                pe.wait_ge(evacs, at.evacs)
                turn_rows(t)

            def mix(at, d, n, br):
                for ins in rows_by_columns(hT, [act_bank(0), act_bank(1)]):
                    to_act(ins)
                w = tile(2).rearrange("p (k n) -> p k n", k=4)
                if br == 1:
                    pe.wait_ge(evacs, WHERE[("mla_out", d, 1)].evacs + 1)
                if br == 0:
                    pe.wait_ge(evacs, WHERE[("diff_sub", d, 1)].evacs + 1)
                if br == 2:
                    pe.wait_ge(dve_ops, WHERE[("taps", d)].dve + 15)
                for t in range(2):
                    b = dve_bank()
                    for k in range(4):
                        ins = pe.matmul(b, (ydT, ymT, ycT)[br][:, k, t * P:(t + 1) * P], w[:, k, :],
                                        start=(k == 0), stop=(k == 3))
                    to_dve(ins)
                release(3)

            def mix_turn(at, d):
                pe.wait_ge(dve_ops, at.dve)
                for k in range(KT):
                    turn_tiles(lambda t: mixed[:, t, k * P:(k + 1) * P])

            def out(at, d, n):
                pe.wait_ge(evacs, at.evacs)
                for ins in rows_by_columns(mixedT, [dve_bank(0), dve_bank(1)]):
                    to_dve(ins)
                release(2)

            def ffn_norm(at, d):
                norm(at, d, h_ffn)

            def query(at, d, i):
                hT_ready(WHERE[("query", d, 0)])
                columns_by_tokens(to_act, act_bank)

            def scores(at, d, t):
                pe.wait_ge(evacs, WHERE[("query", d, 7)].evacs + 2)
                keys = tile()
                for i in range(4):
                    b = act_bank()
                    for c in range(4):
                        hp = 4 * i + c
                        ins = pe.matmul(b[:, c * P:(c + 1) * P], queryT[:, hp, t * P:(t + 1) * P],
                                        keys[:, hp * P:(hp + 1) * P], start=True, stop=True)
                    to_act(ins)
                if t:
                    release(1)

            stage = dict(ple_norm=ple_norm, ple_out=ple_out, x_norm=x_norm, qkv=qkv, latent=latents, conv_c=conv,
                         conv_x=conv_x, conv_b=conv, taps=nothing, diff_norm=nothing, diff_turn=diff_turn,
                         diff_scores=diff_scores, diff_apply=diff_apply, diff_sub=diff_sub, mla_norm=mla_norm,
                         mla_up=mla_up, mla_qk=nothing, mla_turn=mla_turn, mla_scores=mla_scores,
                         mla_apply=mla_apply, mla_out=mla_out, mix_first=mix, mix_more=mix, mix_turn=mix_turn,
                         out=out, ffn_norm=ffn_norm, query=query, scores=scores, topk=nothing)
            rows = Rows()

            def group(step, phase, g, begin=False, end=False):
                filled = turns_before(step, phase)
                for r in range(V_BY_PE):
                    pe.wait_ge(diag_ready, g * V_BY_PE + (pe_rows_before(step, phase) + r + 1))
                    pe.wait_ge(landed[r], (g + (filled + 1)) * 16)
                    for half in range(2):
                        ins = pe.matmul(ps_sum[:, half, :], diag[:, r, :], ring[:, r, half * 512:(half + 1) * 512],
                                        start=(begin and r == 0), stop=(end and r == V_BY_PE - 1))
                    ins.then_inc(pe_rows, 1)

            def serve(n):
                for phase, first, m in rows.parts(n):
                    step = rows.step
                    if PHASES[phase] == "U":
                        continue
                    if first == 0:
                        if 2 * step + phase // 2:
                            pe.wait_ge(sum_added, 2 * step + phase // 2)
                        group(step, phase, 0, begin=True)
                        first, m = 1, m - 1
                    ends = first + m == GROUPS and m > 0
                    m -= ends
                    if m > 1:
                        with pe.Fori(0, m) as i:
                            group(step, phase, i + first)
                    elif m == 1:
                        group(step, phase, first)
                    if ends:
                        group(step, phase, GROUPS - 1, end=True)

            pe.wait_ge(consts_loaded, 16 * N_CONSTS)
            for step, row, rest in PLAN:
                rows.step, rows.pos = step, 0
                for (name, d, *more), at, groups in row:
                    assert (n_act, n_dve, n_tile) == (at.evacs, at.taken, at.tile), (name, d, more)
                    stage[name](at, d, *more)
                    serve(groups)
                serve(rest)


def _tiles(w, k, n):
    kk, nn = w.shape[0] // (k * P), w.shape[1] // n
    return w.reshape(kk, k, P, nn, n).transpose(0, 3, 2, 1, 4).reshape(kk, nn, P, k * n)


def _layer_weights(w, layer):
    out = np.zeros((NT_PLE + NT_DENSE, P, 2048), np.float32)
    at = 0

    def put(tile):
        nonlocal at
        out[at, :, :tile.shape[1]] = tile
        at += 1

    def by_rows(m, n):
        for kh in range(2):
            put(_tiles(m, 4, 512)[kh, n])

    for n in range(2):
        by_rows(w["w_ple_gate"][layer], n)
        put(_tiles(w["w_ple_proj"][layer], 2, 512)[0, n])
    w_in = w["w_in"][layer]
    for n in range(3):
        by_rows(w_in[:, 0:1536], n)
    lat = np.zeros((D, 512), np.float32)
    lat[:, :LATENT] = w_in[:, 1536:1536 + LATENT]
    by_rows(lat, 0)
    first = 1536 + LATENT
    for part in (1, 2, 0):
        cut = _tiles(w_in[:, first + 512 * part:first + 512 * (part + 1)], KT, 256)
        put(cut[0, 0])
        put(cut[0, 1])
    first += 3 * 512
    put(_tiles(w["w_uq"][layer], 2, 768)[0, 0])
    put(w["w_ukv"][layer])
    for n in range(2):
        for br, name in enumerate(("w_br_diff", "w_br_mla", "w_br_conv")):
            by_rows(w_in[:, first + D * br:first + D * (br + 1)], n)
            put(_tiles(w[name][layer], 4, 512)[0, n])
    for n in range(2):
        by_rows(w["w_out"][layer], n)
    cut = _tiles(w["w_query"][layer], KT, 256)
    for i in range(HP // 2):
        put(cut[0, i])
    put(w["sub_keys"][layer].transpose(3, 1, 0, 2).reshape(P, HP * P))
    assert at == len(out)
    return out


def _layer_columns(w, layer):
    def split(v):
        return v.reshape(-1, P).T

    return np.concatenate([
        split(w["g_mix"][layer]), split(w["g_ple"][layer]),
        np.tile(w["g_diff_q"][layer], 2)[:, None], np.tile(w["g_diff_k"][layer], 2)[:, None],
        w["g_diff_sub"][layer][:, None], split(w["g_cq"][layer]), split(w["g_ckv"][layer]),
        w["conv_w"][layer].reshape(-1, P).T], axis=1)


def _everywhere(v):
    return np.ascontiguousarray(np.broadcast_to(v, (P, *v.shape)))


def kernel(**inputs):
    from concourse import bacc
    from concourse.bass_utils import run_bass_kernel_spmd

    w = {k: np.asarray(v) for k, v in inputs.items()}
    half = MROPE // 2
    angle = np.arange(SEQ, dtype=np.float32)[:, None] * (
        10000.0 ** (-np.arange(half, dtype=np.float32) / half)).astype(np.float32)[None, :]
    cos = np.concatenate([np.cos(angle), np.cos(angle)], axis=1)
    sin = np.concatenate([-np.sin(angle), np.sin(angle)], axis=1)
    arrays = {
        "x": w["x"].reshape(4, P, D),
        "pT": w["p"].reshape(DEPTH, SEQ, 2, P).transpose(0, 3, 2, 1),
        "weights": np.stack([_layer_weights(w, layer) for layer in range(DEPTH)]),
        "cols": np.stack([_layer_columns(w, layer) for layer in range(DEPTH)], axis=1),
        "ffn_rows": np.stack([_everywhere(w["g_ffn"][layer]) for layer in range(DEPTH)]),
        "mla_rows": _everywhere(np.stack([w["g_mla_q"], w["g_mla_k"]], axis=1)),
        "lam": _everywhere(np.stack([w["lam_q1"], w["lam_k1"], w["lam_q2"], w["lam_k2"]], axis=1)),
        "rope": np.stack([cos, sin]).reshape(2, 4, P, MROPE).transpose(0, 2, 1, 3).astype(np.float32),
        "ident": np.eye(P, dtype=np.float32),
        **{f"u{layer}": w["u_experts"][layer] for layer in range(DEPTH)},
        **{f"v{layer}": w["v_experts"][layer] for layer in range(DEPTH)},
    }
    arrays = {"in_" + k: np.ascontiguousarray(v) for k, v in arrays.items()}
    nc = bacc.Bacc("TRN2", target_bir_lowering=False, num_devices=1)
    aps = {k[3:]: nc.dram_tensor(k, v.shape, F32, kind="ExternalInput").ap() for k, v in arrays.items()}
    aps["out"] = nc.dram_tensor("out_x", (4, P, D), F32, kind="ExternalOutput").ap()
    trunk(nc, aps)
    r = run_bass_kernel_spmd(nc, [arrays], core_ids=[0])
    return r.results[0]["out_x"].reshape(1, SEQ, D)
```

```python
from contextlib import ExitStack

import numpy as np

import concourse.bass as bass
from concourse import mybir

F32 = mybir.dt.float32
U32 = mybir.dt.uint32
ALU = mybir.AluOpType
ACT = mybir.ActivationFunctionType
AX = mybir.AxisListType.X

P = 128
D = 1024
SEQ = 512
DEPTH = 2
KT = D // P
HALF = 256
STEPS = DEPTH * SEQ // HALF
EPS = 1e-6
MASKED = -1e30
LOWEST = -3e38
DH, DHD = 4, 64
MH, MQK, MNOPE, MROPE, MV = 8, 96, 64, 32, 64
QL, KVL = 256, 128
LATENT = QL + KVL + MROPE
HEADS, TOPK = 8, 16
HP = 2 * HEADS
ROWS = HEADS * TOPK
CANDS = 4 * TOPK + (TOPK - 4) * 4
LAMBDA_INIT = [0.8 - 0.6 * float(np.exp(-0.3 * layer)) for layer in range(DEPTH)]
SLOPES = [2.0 ** (-8.0 * (h + 1) / DH) for h in range(DH)]

RING = 8
UNIT = RING // 2
GROUPS = ROWS // RING
UNITS = 2 * GROUPS
PHASES = ["U", "V", "U", "V"]
PE_SHARE = [0, 2, 0, 2]

COLS = ["g_mix", "g_ple", "g_dq", "g_dk", "g_dsub", "g_cq", "g_ckv", "conv"]
COL_N = dict(g_mix=KT, g_ple=KT, g_dq=1, g_dk=1, g_dsub=1, g_cq=2, g_ckv=1, conv=12)
COL_AT, NCOL = {}, 0
for _name in COLS:
    COL_AT[_name] = NCOL
    NCOL += COL_N[_name]

W_SLOTS = 3
PLE_TILES = [2048, 2048, 1024] * 2
MIX_TILES = [2048, 2048, 2048] * 6
DENSE_TILES = ([2048] * 6 + [2048] * 6 + [2048] * 2 + [1536, 1024] + MIX_TILES + [2048] * 4
               + [2048] * HEADS)
NT_PLE, NT_DENSE = len(PLE_TILES), len(DENSE_TILES)

COUNTS = {
    "ple_norm": (8, 3, 0, 4), "ple_out": (2, 0, 2, 2),
    "x_norm": (8, 3, 0, 4), "qkv": (2, 0, 0, 0), "latent": (2, 0, 0, 0),
    "conv_c": (2, 0, 0, 0), "conv_x": (0, 0, 2, 0), "conv_b": (2, 0, 0, 0), "taps": (0, 0, 0, 15),
    "diff_norm": (0, 1, 0, 5), "diff_turn": (8, 0, 0, 0),
    "diff_scores": (0, 2, 2, 2), "diff_flip": (1, 0, 0, 4), "diff_pv": (1, 0, 0, 0), "diff_sub": (1, 1, 0, 5),
    "mla_norm": (3, 5, 0, 5), "mla_up": (8, 4, 0, 0), "mla_qk": (0, 1, 0, 28), "mla_turn": (16, 0, 0, 0),
    "mla_scores": (0, 1, 1, 1), "mla_flip": (1, 0, 0, 1), "mla_pv": (1, 0, 0, 0), "mla_out": (1, 0, 0, 0),
    "mix_first": (2, 0, 2, 0), "mix_more": (2, 0, 2, 2), "mix_turn": (8, 0, 0, 0), "out": (0, 0, 2, 0),
    "ffn_norm": (8, 3, 0, 4), "query": (2, 0, 0, 0), "scores": (2, 0, 0, 0), "rank": (0, 0, 0, 20),
}
TOPK_OPS = [3, 16, 16, 16, 3, 3, 4]


def counts(stage):
    if stage[0] == "topk":
        part = stage[3]
        return (0, part == len(TOPK_OPS) - 1, 0, TOPK_OPS[part])
    return COUNTS[stage[0]]



COST = {
    "ple_norm": 12, "ple_out": 18, "x_norm": 12, "qkv": 14, "latent": 12, "conv_c": 7, "conv_x": 7,
    "conv_b": 7, "taps": 2, "diff_norm": 12, "diff_turn": 4, "diff_scores": 3, "diff_flip": 3, "diff_pv": 1,
    "diff_sub": 5, "mla_norm": 8, "mla_up": 4, "mla_qk": 12, "mla_turn": 6, "mla_scores": 2,
    "mla_flip": 2, "mla_pv": 1, "mla_out": 1, "mix_first": 21, "mix_more": 21, "mix_turn": 4, "out": 14,
    "ffn_norm": 12, "query": 7, "scores": 1, "rank": 0, "topk": 6,
}
PHASE_ENDS = [("latent",), ("mla_turn",), ("out", 1)]


class At:

    def __init__(self, base, tiles):
        self.evacs, self.act, self.taken, self.dve = base
        self.tile = tiles


def tiles_done(name, at, pairs):
    if name in ("ple_out", "mix_first", "mix_more"):
        return [("w_used", pairs + 1), ("for_act", at.evacs + 2), ("for_dve", at.taken + 2)]
    if name in ("qkv", "latent"):
        return [("w_used", pairs + 1), ("for_act", at.evacs + 2)]
    if name == "out":
        return [("w_used", pairs + 1), ("for_dve", at.taken + 2)]
    if name == "mla_up":
        return [("for_act", at.evacs + 8)] * 2
    if name == "conv_x":
        return [("for_dve", at.taken + 2)]
    return [("for_act", at.evacs + 2)]


def choice(d, t):
    return [("topk", d, t, part) for part in range(len(TOPK_OPS))]


def attention(kind, d, heads):
    out, n = [], 2 * heads
    for i in range(n + 3):
        if i < n:
            out.append((kind + "_scores", d, i))
        if 2 <= i < n + 2:
            out.append((kind + "_flip", d, i - 2))
        if i >= 3:
            out.append((kind + "_pv", d, i - 3))
    return out


def stages_of(step):
    out = []
    done = step - 1
    if step == 0:
        out += choice(0, 1)
    if done >= 0:
        out += [("ple_norm", done)] + [("ple_out", done, n) for n in range(2)]
    d = step + 1
    if d < STEPS:
        out += [("x_norm", d), ("conv_c", d, 0), ("conv_c", d, 1), ("conv_x", d, 0), ("conv_x", d, 1),
                ("conv_b", d, 0), ("conv_b", d, 1), ("taps", d)]
        out += [("qkv", d, 0), ("qkv", d, 1), ("diff_norm", d), ("qkv", d, 2), ("latent", d), ("diff_turn", d)]
        out += attention("diff", d, DH)
        out += [("diff_sub", d, t) for t in range(2)]
        out += [("mla_norm", d), ("mla_up", d), ("mla_qk", d), ("mla_turn", d)]
        out += attention("mla", d, MH)
        out += [("mla_out", d, t) for t in range(2)]
        for n in range(2):
            out += [("mix_first", d, n, 0), ("mix_more", d, n, 1), ("mix_more", d, n, 2)]
        out += [("mix_turn", d), ("out", d, 0), ("out", d, 1), ("ffn_norm", d)]
        for i in range(HEADS + 1):
            out += [("query", d, i)] if i < HEADS else []
            out += [("scores", d, i - 1), ("rank", d, i - 1)] if i else []
        out += choice(d, 0)
        if d:
            out += choice(d, 1)
    return out


TILES_OF = {"ple_out": 3, "qkv": 2, "latent": 2, "conv_c": 1, "conv_x": 1, "conv_b": 1, "mla_up": 2,
            "mix_first": 3, "mix_more": 3, "out": 2, "query": 1}


def timeline():
    base, tile, plan, where, done, pairs = [0, 0, 0, 0], 0, [], {}, [], 0
    for step in range(-1, STEPS + 1):
        row, served = [], 0
        stages = stages_of(step)
        phase_of, phase = [], 0
        for i, st in enumerate(stages):
            phase_of.append(phase)
            if phase < 3 and (st[0], *st[2:]) == PHASE_ENDS[phase]:
                phase += 1
        whole = [sum(COST[st[0]] for st, q in zip(stages, phase_of) if q == p) for p in range(4)]
        spent = [0.0] * 4
        for st, phase in zip(stages, phase_of):
            at = At(tuple(base), tile)
            where[st] = at
            base = [a + b for a, b in zip(base, counts(st))]
            tiles = TILES_OF.get(st[0], 0)
            if tiles:
                tile += tiles
                done += tiles_done(st[0], at, pairs)
                pairs = max([n for name, n in done if name == "w_used"], default=0)
            spent[phase] += COST[st[0]]
            units = 0
            if 0 <= step < STEPS:
                goal = phase * UNITS + int(UNITS * spent[phase] / whole[phase] + 1e-9)
                units = max(0, goal - served)
                served += units
            row.append((st, at, units))
        plan.append((step, row, 4 * UNITS - served if 0 <= step < STEPS else 0))
    return plan, where, done


PLAN, WHERE, TILE_DONE = timeline()


class Rows:

    def __init__(self):
        self.step, self.pos = -1, 0

    def ahead(self, n):
        phase, first = divmod(self.pos, UNITS)
        return min(n, 2, UNITS - first) if first and PHASES[phase % 4] == "V" else 0

    def parts(self, n):
        while n:
            phase, first = divmod(self.pos, UNITS)
            m = min(n, UNITS - first)
            yield phase, first, m
            self.pos += m
            n -= m


def pieces(first, m):
    end = first + m
    while first < end:
        groups = (min(end, UNITS - 2) - first) // 2
        if first % 2 or first == 0 or groups < 2:
            yield first, 0
            first += 1
        else:
            yield first, groups
            first += 2 * groups


def dve_rows_before(step, phase):
    per = [UNITS * (UNIT - share) for share in PE_SHARE]
    return step * sum(per) + sum(per[:phase])


def pe_rows_before(step, phase):
    per = [UNITS * share for share in PE_SHARE]
    return step * sum(per) + sum(per[:phase])


def turns_before(step, phase):
    return (step * 4 + phase) * GROUPS


def trunk(nc, a):
    ctx = ExitStack()
    with ctx:
        def sb(name, shape, dt=F32):
            return ctx.enter_context(nc.sbuf_tensor(name, shape, dt))

        def sem(name):
            return ctx.enter_context(nc.semaphore(name))

        x = sb("x", [P, 4, D])
        diff_v = sb("diff_v", [P, 4, 512])
        diff_kT = sb("diff_kT", [P, DH, SEQ])
        mla_kT = sb("mla_kT", [P, MH, SEQ])
        mla_v = sb("mla_v", [P, 4, 512])
        h_ffn = sb("h_ffn", [P, 2, D])
        ring = sb("ring", [P, RING, D])
        wt = sb("wt", [P, W_SLOTS, 2048])
        dist = sb("dist", [P, 512])
        mask = sb("mask", [P, 512])
        ident = sb("ident", [P, P])
        diag = sb("diag", [P, 2 * max(PE_SHARE), P])
        cols = sb("cols", [P, DEPTH, NCOL])
        ffn_row = sb("ffn_row", [P, D])
        mla_rows = sb("mla_rows", [P, DEPTH, 2, MQK])
        rope_cos = sb("rope_cos", [P, 4, MROPE])
        rope_sin = sb("rope_sin", [P, 4, MROPE])
        iota = sb("iota", [P, TOPK])
        pT = sb("pT", [P, 2, HALF])
        experts = sb("experts", [P, 2, 2, ROWS], U32)
        gate = sb("gate", [P, 2, 2, ROWS])
        staged = sb("staged", [P, 2, RING], U32)
        dots = sb("dots", [P, ROWS])
        weight = sb("weight", [P, ROWS])
        tail = sb("tail", [P, 4, 2])
        lam = sb("lam", [P, DEPTH, 4])
        dq_gain = sb("dq_gain", [P, DEPTH])
        dsub_gain = sb("dsub_gain", [P, DEPTH])
        stats = sb("stats", [P, 128])
        scratch = sb("scratch", [P, 512])

        area_h = sb("area_h", [P, 2048])
        area_b = sb("area_b", [P, 5120])
        area_e = sb("area_e", [P, 2048])
        area_f = sb("area_f", [P, 1024])
        area_y = sb("area_y", [P, 2, 512])
        area_t = sb("area_t", [P, 3072])
        latent = sb("latent", [P, 2, LATENT])

        hT = area_h[:, :].rearrange("p (k t) -> p k t", k=KT)
        normed = area_b[:, 0:2048].rearrange("p (t n) -> p t n", t=2)
        z = area_b[:, 0:2048].rearrange("p (c t n) -> p c t n", c=2, t=2)
        qm = area_b[:, 0:1536].rearrange("p (t h d) -> p t h d", t=2, h=MH)
        km = area_b[:, 1536:3072].rearrange("p (t h d) -> p t h d", t=2, h=MH)
        diff_qT = area_b[:, 3072:4096].rearrange("p (h t) -> p h t", h=DH)
        mla_qT = area_b[:, 3072:5120].rearrange("p (h t) -> p h t", h=MH)
        mixed = normed
        mixedT = area_b[:, 3072:5120].rearrange("p (k t) -> p k t", k=KT)
        queryT = area_b[:, 0:4096].rearrange("p (c t) -> p c t", c=HP)
        squares = area_e[:, :]
        conv_cT = area_e[:, 0:1024].rearrange("p (c t) -> p c t", c=4)
        conv_bT = area_e[:, 1024:2048].rearrange("p (c t) -> p c t", c=4)
        diff_prob = [area_e[:, 0:1024], area_e[:, 1024:2048], area_b[:, 2048:3072]]
        diff_prob = [b.rearrange("p (m k) -> p m k", m=2) for b in diff_prob]
        mla_prob = [area_e[:, 512 * b:512 * (b + 1)] for b in range(4)]
        gates = area_e[:, :].rearrange("p (b t n) -> p b t n", b=2, t=2)
        key_scores = area_e[:, :].rearrange("p (c n) -> p c n", c=HP)
        cqT = area_f[:, 0:512].rearrange("p (k t) -> p k t", k=2)
        ckvT = area_f[:, 512:768]
        probT = area_f[:, :].rearrange("p (b k q) -> p b k q", b=2, q=P)
        product = area_f[:, :].rearrange("p (t n) -> p t n", t=2)
        ydT = area_t[:, 0:1024].rearrange("p (k t) -> p k t", k=4)
        ymT = area_t[:, 1024:2048].rearrange("p (k t) -> p k t", k=4)
        ycT = area_t[:, 2048:3072].rearrange("p (k t) -> p k t", k=4)
        conv_u = area_t[:, 0:4 * (HALF + 2)].rearrange("p (k t) -> p k t", k=4)
        cand = area_t[:, 0:2048]
        top_v = area_t[:, 2048:2560].rearrange("p (t c k) -> p t c k", t=2, c=HP)
        top_i = area_t[:, 2560:3072].bitcast(U32).rearrange("p (t c k) -> p t c k", t=2, c=HP)
        sub_keys = [area_y[:, :, :].rearrange("p c n -> p (c n)"), area_f[:, :]]
        top_f = area_h[:, 512:768].rearrange("p (h c k) -> p h c k", h=HEADS, c=2)
        best_v = area_h[:, 768:896].rearrange("p (h k) -> p h k", h=HEADS)
        best_c = area_h[:, 896:1024].bitcast(U32).rearrange("p (h k) -> p h k", h=HEADS)
        part_u = area_h[:, 1024:1280].bitcast(U32).rearrange("p (c k) -> p c k", c=2)
        part_f = area_h[:, 1280:1536].rearrange("p (c h k) -> p c h k", c=2, h=HEADS)
        part_i = area_h[:, 1536:1792].rearrange("p (c k) -> p c k", c=2)
        exps = area_h[:, 1792:1920].rearrange("p (h k) -> p h k", h=HEADS)
        lam_in = area_b[:, 4096:4096 + 4 * DHD * DEPTH].rearrange("p (l c d) -> p l c d", l=DEPTH, c=4)
        ss = stats[:, 0:32]
        mean_sq = stats[:, 32:64]
        root = stats[:, 64:96]
        soft = sb("soft", [P, 5, 4, 2])
        top, neg_top, total, inv, inv_lam = (soft[:, i, :, :] for i in range(5))
        rstd = sb("rstd", [P, 32])
        esum = stats[:, 114:122]
        ss_rope = stats[:, 122:124]

        ps_act = ctx.enter_context(nc.psum_tensor("ps_act", [P, 3, 512], F32))
        ps_dve = ctx.enter_context(nc.psum_tensor("ps_dve", [P, 3, 512], F32))
        ps_sum = ctx.enter_context(nc.psum_tensor("ps_sum", [P, 2, 512], F32))

        consts_loaded = sem("consts_loaded")
        x_loaded = [sem(f"x_loaded{i}") for i in range(2)]
        setup_done = sem("setup_done")
        row_loaded = sem("row_loaded")
        pT_loaded = sem("pT_loaded")
        w_loaded = [sem(f"w_loaded{i}") for i in range(W_SLOTS)]
        w_used = sem("w_used")
        keys_loaded = sem("keys_loaded")
        consts_made = sem("consts_made")
        for_act = sem("bank_for_act")
        for_dve = sem("bank_for_dve")
        evacs = sem("evacs")
        act_ops = sem("act_ops")
        taken = sem("taken")
        dve_ops = sem("dve_ops")
        experts_ready = sem("experts_ready")
        staged_ready = sem("staged_ready")
        turn = sem("pool_turn")
        landed = [sem(f"landed{i}") for i in range(RING)]
        dve_rows = sem("dve_rows")
        pe_rows = sem("pe_rows")
        diag_ready = sem("diag_ready")
        gelu_ready = sem("gelu_ready")
        weight_ready = sem("weight_ready")
        sum_added = sem("sum_added")
        stored = sem("stored")

        def col(name, layer, i=0):
            j = COL_AT[name] + i
            return cols[:, layer, j:j + 1]

        block = ctx.enter_context(nc.Block())
        N_CONSTS = 6

        @block.sync
        def _(sp):
            sp.dma_start(ident[:, :], a["ident"]).then_inc(consts_loaded, 16)
            sp.dma_start(cols[:, :, :], a["cols"]).then_inc(consts_loaded, 16)
            for t in range(2):
                sp.dma_start(x[:, t, :], a["x"][t]).then_inc(x_loaded[t // 2], 16)
            sp.dma_start(lam_in, a["lam"]).then_inc(consts_loaded, 16)
            sp.dma_start(mla_rows[:, :, :, :], a["mla_rows"]).then_inc(consts_loaded, 16)
            sp.dma_start(rope_cos[:, :, :], a["rope"][0]).then_inc(consts_loaded, 16)
            sp.dma_start(rope_sin[:, :, :], a["rope"][1]).then_inc(consts_loaded, 16)
            sp.dma_start(ffn_row[:, :], a["ffn_rows"][0]).then_inc(row_loaded, 16)
            tile = 0

            def load(layer, first, widths):
                nonlocal tile
                for i, width in enumerate(widths):
                    if tile >= W_SLOTS:
                        name, count = TILE_DONE[tile - W_SLOTS]
                        sp.wait_ge({"w_used": w_used, "for_act": for_act, "for_dve": for_dve}[name], count)
                    sp.dma_start(wt[:, tile % W_SLOTS, 0:width], a["weights"][layer, first + i, :, 0:width])\
                        .then_inc(w_loaded[tile % W_SLOTS], 16)
                    tile += 1

            for step in range(-1, STEPS + 1):
                done, d = step - 1, step + 1
                if done >= 0:
                    if done >= 1:
                        sp.wait_ge(for_dve, WHERE[("ple_out", done - 1, 1)].taken + 2)
                    half = done % 2
                    sp.dma_start(pT[:, :, :], a["pT"][done // 2, :, :, half * HALF:(half + 1) * HALF])\
                        .then_inc(pT_loaded, 16)
                    load(done // 2, 0, PLE_TILES)
                if d == 0:
                    load(0, NT_PLE, DENSE_TILES[:4])
                    for t in range(2, 4):
                        sp.dma_start(x[:, t, :], a["x"][t]).then_inc(x_loaded[t // 2], 16)
                    load(0, NT_PLE + 4, DENSE_TILES[4:-HEADS])
                elif d < STEPS:
                    if d == 2:
                        sp.wait_ge(dve_ops, WHERE[("ffn_norm", 1)].dve + 4)
                        sp.dma_start(ffn_row[:, :], a["ffn_rows"][1]).then_inc(row_loaded, 16)
                    load(d // 2, NT_PLE, DENSE_TILES[:-HEADS])
                if d < STEPS:
                    sp.wait_ge(evacs, WHERE[("mla_out", d, 1)].evacs + 1)
                    sp.wait_ge(dve_ops, WHERE[("mix_more", d, 1, 2)].dve + 2)
                    for i in range(2):
                        sp.dma_start(sub_keys[i], a["keys"][d // 2, i]).then_inc(keys_loaded, 16)
                    load(d // 2, NT_PLE + NT_DENSE - HEADS, DENSE_TILES[-HEADS:])
                if done >= 2:
                    sp.wait_ge(dve_ops, WHERE[("ple_out", done, 1)].dve + 2)
                    for t in range(2):
                        sp.dma_start(a["out"][2 * (done % 2) + t], x[:, 2 * (done % 2) + t, :]).then_inc(stored, 16)
            sp.wait_ge(stored, 16 * 4)

        @block.gpsimd
        def _(pool):
            pool.iota(dist[:, :], [[1, 512]], base=-384, channel_multiplier=-1,
                      allow_small_or_imprecise_dtypes=True).then_inc(consts_made, 1)
            pool.memset(mask[:, :], 0.0).then_inc(consts_made, 1)
            pool.iota(iota[:, :], [[1, TOPK]], base=0, channel_multiplier=0,
                      allow_small_or_imprecise_dtypes=True).then_inc(consts_made, 1)
            pool.wait_ge(consts_made, 3)
            for m in (dist, mask):
                pool.affine_select(out=m[:, :], in_=m[:, :], compare_op=ALU.is_ge, fill=MASKED, base=384,
                                   pattern=[[-1, 512]], channel_multiplier=1).then_inc(consts_made, 1)
            n_staged = 0

            def group(step, phase, t, first, half, reg):
                table = a[f"{PHASES[phase].lower()}{step // 2}"]
                g = first if reg is None else first + 2 * reg
                columns = slice(g * RING, (g + 1) * RING) if reg is None else bass.ds(g * RING, RING)
                pool.tensor_copy(staged[:, half, :], experts[:, step % 2, t, columns]).then_inc(staged_ready, 1)
                pool.wait_ge(staged_ready, n_staged + 1 if reg is None else reg * 2 + (n_staged + 1))
                pool.sem_inc(turn, 1)
                before = (step, phase) if (first or reg is not None) else (step - (phase == 0), (phase - 1) % 4)
                for r in range(RING):
                    if before[0] >= 0:
                        half_turn, k = divmod(r, UNIT)
                        pe_share = PE_SHARE[before[1]]
                        dve_share = UNIT - pe_share
                        if k < pe_share:
                            by_dve, per, k = False, 2 * pe_share, half_turn * pe_share + k
                        else:
                            by_dve, per, k = True, 2 * dve_share, half_turn * dve_share + k - pe_share
                        rows_before = dve_rows_before(*before) if by_dve else pe_rows_before(*before)
                        count = rows_before + k + 1
                        if before == (step, phase):
                            count = count + (g - 1) * per
                        else:
                            count = count + (GROUPS - 1) * per
                        pool.wait_ge(dve_rows if by_dve else pe_rows, count)
                        pool.sem_inc(turn, 1)
                    pool.indirect_dma_start(
                        ring[:, r, :], None, table[:, :],
                        bass.IndirectOffsetOnAxis(ap=staged[:, half, r:r + 1], axis=0)).then_inc(landed[r], 16)

            for step in range(STEPS):
                for phase in range(4):
                    t = phase // 2
                    pool.wait_ge(experts_ready, 2 * step + t + 1)
                    group(step, phase, t, 0, 0, None)
                    n_staged += 1
                    with pool.Fori(0, GROUPS // 2 - 1) as i:
                        group(step, phase, t, 1, 1, i)
                        n_staged += 1
                        group(step, phase, t, 2, 0, i)
                        n_staged -= 1
                    n_staged += GROUPS - 2
                    group(step, phase, t, GROUPS - 1, 1, None)
                    n_staged += 1

        @block.scalar
        def _(act):
            n_bank = 0
            n_evac = 0
            n_op = 0

            def evac(out, in_, func=ACT.Copy, scale=1.0, last=True):
                nonlocal n_bank, n_evac, n_op
                act.wait_ge(for_act, n_bank + 1)
                ins = act.activation(out, in_, func, scale=scale)
                if last:
                    n_bank += 1
                    n_evac += 1
                    ins.then_inc(evacs, 1)
                else:
                    n_op += 1
                    ins.then_inc(act_ops, 1)

            def bank(width=512):
                return ps_act[:, n_bank % 3, 0:width]

            def op(*args, **kw):
                nonlocal n_op
                act.activation(*args, **kw).then_inc(act_ops, 1)
                n_op += 1

            def square_sums(at, d):
                g0 = 2 * (d % 2)
                for t in range(2):
                    if t:
                        act.wait_ge(act_ops, n_op)
                    op(squares[:, 0:D], x[:, g0 + t, :], ACT.Square, accum_out=ss[:, t:t + 1])
                act.wait_ge(dve_ops, at.dve + 1)
                op(root[:, 0:2], mean_sq[:, 0:2], ACT.Sqrt)

            def norm(at, d, gain):
                act.wait_ge(dve_ops, at.dve)
                act.wait_ge(taken, at.taken)
                act.wait_ge(act_ops, at.act)
                act.wait_ge(evacs, at.evacs)
                square_sums(at, d)
                for k in range(KT):
                    evac(hT[:, k, :], bank(HALF), scale=1.0 if gain is None else col(gain, d // 2, k))

            def ple_norm(at, d):
                act.wait_ge(sum_added, 2 * d + 2)
                norm(at, d, "g_ple")

            def ple_out(at, d, n):
                for t in range(2):
                    act.wait_ge(taken, at.taken)
                    evac(gates[:, n, t, :], bank(), ACT.Sigmoid)

            def x_norm(at, d):
                if d < 2:
                    act.wait_ge(x_loaded[d], 16 * 2)
                norm(at, d, "g_mix")

            def qkv(at, d, n):
                for t in range(2):
                    out = diff_v[:, 2 * (d % 2) + t, :] if n == 2 else z[:, n, t, :]
                    evac(out, bank())

            def latents(at, d):
                for t in range(2):
                    evac(latent[:, t, :], bank(LATENT))

            def conv_c(at, d, i):
                act.wait_ge(act_ops, at.act)
                for c in range(2):
                    evac(conv_cT[:, 2 * i + c, :], bank(HALF))

            def conv_x(at, d, i):
                pass

            def conv_b(at, d, i):
                for c in range(2):
                    evac(conv_bT[:, 2 * i + c, :], bank(HALF))

            def taps(at, d):
                pass

            def diff_norm(at, d):
                act.wait_ge(dve_ops, at.dve + 3)
                op(root[:, 0:32], mean_sq[:, 0:32], ACT.Sqrt)

            def diff_turn(at, d):
                g0 = 2 * (d % 2)
                for h in range(DH):
                    evac(diff_qT[:, h, :], bank(HALF), scale=dq_gain[:, d // 2:d // 2 + 1])
                    evac(diff_kT[:, h, g0 * P:g0 * P + HALF], bank(HALF), scale=col("g_dk", d // 2))

            def width_of(d, t):
                return (2 * (d % 2) + t + 1) * P

            def diff_scores(at, d, i):
                b, w = i % 3, width_of(d, i // DH)
                act.wait_ge(dve_ops, at.dve + 2)
                for m in range(2):
                    p = diff_prob[b][:, m, 0:w]
                    op(p, p, ACT.Exp, bias=neg_top[:, b, m:m + 1], accum_out=total[:, b, m:m + 1])

            def diff_flip(at, d, i):
                w = width_of(d, i // DH)
                evac(probT[:, i % 2, 0:w // P, :].rearrange("p k q -> p (k q)"), bank(w))

            def diff_pv(at, d, i):
                t, h = divmod(i, DH)
                evac(area_y[:, t, h * P:(h + 1) * P], bank(P))

            def diff_sub(at, d, t):
                act.wait_ge(dve_ops, at.dve + 3)
                op(root[:, 0:4], mean_sq[:, 0:4], ACT.Sqrt)
                evac(ydT[:, :, t * P:(t + 1) * P], bank().rearrange("p (k t) -> p k t", k=4),
                     scale=dsub_gain[:, d // 2:d // 2 + 1])

            def mla_norm(at, d):
                act.wait_ge(evacs, at.evacs)
                for t in range(2):
                    for i, (lo, hi) in enumerate(((0, QL), (QL, QL + KVL))):
                        op(area_e[:, (2 * t + i) * 256:(2 * t + i) * 256 + hi - lo], latent[:, t, lo:hi], ACT.Square,
                           accum_out=ss[:, 2 * i + t:2 * i + t + 1])
                act.wait_ge(dve_ops, at.dve + 2)
                op(root[:, 0:4], mean_sq[:, 0:4], ACT.Sqrt)
                for k in range(2):
                    evac(cqT[:, k, :], bank(HALF), scale=col("g_cq", d // 2, k))
                evac(ckvT, bank(HALF), scale=col("g_ckv", d // 2))

            def mla_up(at, d):
                for t in range(2):
                    row = qm[:, t, :, :].rearrange("p h d -> p (h d)")
                    evac(row[:, 0:512], bank())
                    evac(row[:, 512:768], bank(256))
                    for i in range(2):
                        part = bank().rearrange("p (h d) -> p h d", h=4)
                        evac(km[:, t, 4 * i:4 * i + 4, 0:MNOPE], part[:, :, 0:MNOPE], last=False)
                        evac(mla_v[:, 2 * (d % 2) + t, 256 * i:256 * (i + 1)].rearrange("p (h d) -> p h d", h=4),
                             part[:, :, MNOPE:MNOPE + MV])

            def mla_qk(at, d):
                act.wait_ge(dve_ops, at.dve + 8)
                op(root[:, 0:32], mean_sq[:, 0:32], ACT.Sqrt)

            def mla_turn(at, d):
                g0 = 2 * (d % 2)
                for h in range(MH):
                    evac(mla_qT[0:MQK, h, :], bank(HALF)[0:MQK], scale=float(MQK) ** -0.5)
                    evac(mla_kT[0:MQK, h, g0 * P:g0 * P + HALF], bank(HALF)[0:MQK])

            def mla_scores(at, d, i):
                b, w = i % 4, width_of(d, i // MH)
                act.wait_ge(dve_ops, at.dve + 1)
                p = mla_prob[b][:, 0:w]
                op(p, p, ACT.Exp, bias=neg_top[:, b, 0:1], accum_out=total[:, b, 0:1])

            def mla_flip(at, d, i):
                w = width_of(d, i // MH)
                evac(probT[:, i % 2, 0:w // P, :].rearrange("p k q -> p (k q)"), bank(w))

            def mla_pv(at, d, i):
                t, h = divmod(i, MH)
                act.wait_ge(dve_ops, WHERE[("mla_flip", d, i)].dve + 1)
                evac(area_y[:, t, h * MV:(h + 1) * MV], bank(MV), scale=inv[:, i % 4, 0:1])

            def mla_out(at, d, t):
                evac(ymT[:, :, t * P:(t + 1) * P], bank().rearrange("p (k t) -> p k t", k=4))

            def mix(at, d, n, br):
                for t in range(2):
                    act.wait_ge(taken, at.taken - (2 if br or n else 0))
                    if not (br or n):
                        act.wait_ge(act_ops, at.act)
                    evac(gates[:, (3 * n + br) % 2, t, :], bank(), ACT.Sigmoid)

            def mix_turn(at, d):
                for k in range(KT):
                    evac(mixedT[:, k, :], bank(HALF))

            def out(at, d, n):
                pass

            def ffn_norm(at, d):
                norm(at, d, None)

            def query(at, d, i):
                for c in range(2):
                    evac(queryT[:, 2 * i + c, :], bank(HALF))

            def scores(at, d, i):
                act.wait_ge(act_ops, at.act)
                if i >= 4:
                    act.wait_ge(dve_ops, WHERE[("rank", d, i - 4)].dve + 20)
                else:
                    act.wait_ge(dve_ops, WHERE[("query", d, 0)].dve)
                for t in range(2):
                    first = 4 * (i % 4) + 2 * t
                    evac(key_scores[:, first:first + 2, :].rearrange("p c n -> p (c n)"), bank(2 * P))

            def nothing(at, d, *more):
                pass

            def topk(at, d, t, part):
                if part == len(TOPK_OPS) - 1:
                    act.wait_ge(dve_ops, at.dve + 1)
                    op(exps, exps, ACT.Exp)

            stage = dict(ple_norm=ple_norm, ple_out=ple_out, x_norm=x_norm, qkv=qkv, latent=latents, conv_c=conv_c,
                         conv_x=conv_x, conv_b=conv_b, taps=taps, diff_norm=diff_norm, diff_turn=diff_turn,
                         diff_scores=diff_scores, diff_flip=diff_flip, diff_pv=diff_pv, diff_sub=diff_sub, mla_norm=mla_norm,
                         mla_up=mla_up, mla_qk=mla_qk, mla_turn=mla_turn, mla_scores=mla_scores,
                         mla_flip=mla_flip, mla_pv=mla_pv, mla_out=mla_out, mix_first=mix, mix_more=mix, mix_turn=mix_turn,
                         out=out, ffn_norm=ffn_norm, query=query, scores=scores, rank=nothing, topk=topk)
            rows = Rows()

            def make_diag(step, phase, g, half):
                share, former = PE_SHARE[phase], pe_rows_before(step, phase)
                for k in range(share):
                    j, i = g * RING + (half * UNIT + k), half * share + k
                    if not isinstance(g, int) or g:
                        act.wait_ge(pe_rows, (g - 1) * (2 * share) + (former + i + 1))
                    elif former:
                        act.wait_ge(pe_rows, former)
                    column = weight[:, j:j + 1] if isinstance(g, int) else weight[:, bass.ds(j, 1)]
                    act.activation(diag[:, i, :], ident[:, :], ACT.Copy, scale=column).then_inc(diag_ready, 1)

            def serve(n):
                for phase, first, m in rows.parts(n):
                    step = rows.step
                    if PHASES[phase] == "U":
                        if first + m == UNITS:
                            act.wait_ge(dve_rows, dve_rows_before(step, phase) + ROWS)
                            act.activation(dots[:, :], dots[:, :], ACT.Gelu).then_inc(gelu_ready, 1)
                        continue
                    if first == 0:
                        act.wait_ge(weight_ready, 2 * step + phase // 2 + 1)
                    for unit, groups in pieces(first, m):
                        if groups:
                            with act.Fori(0, groups) as i:
                                make_diag(step, phase, i + unit // 2, 0)
                                make_diag(step, phase, i + unit // 2, 1)
                        else:
                            make_diag(step, phase, unit // 2, unit % 2)

            act.wait_ge(consts_loaded, 16 * N_CONSTS)
            act.wait_ge(consts_made, 5 + 1)
            act.activation(lam[:, :, 0:2], lam[:, :, 0:2], ACT.Exp).then_inc(consts_made, 1)
            for step, row, rest in PLAN:
                rows.step, rows.pos = step, 0
                for (name, d, *more), at, units in row:
                    assert (n_evac, n_op) == (at.evacs, at.act), (name, d, more, n_evac, n_op, at.evacs, at.act)
                    ahead = rows.ahead(units)
                    serve(ahead)
                    stage[name](at, d, *more)
                    serve(units - ahead)
                serve(rest)

        @block.vector
        def _(dve):
            n_bank = 0
            n_op = 0

            def op(ins):
                nonlocal n_op
                ins.then_inc(dve_ops, 1)
                n_op += 1

            def take(ins):
                nonlocal n_bank
                ins.then_inc(taken, 1)
                n_bank += 1

            def bank(width=512):
                dve.wait_ge(for_dve, n_bank + 1)
                return ps_dve[:, n_bank % 3, 0:width]

            def link():
                dve.wait_ge(dve_ops, n_op)

            def mean(out, in_, n):
                op(dve.tensor_scalar(out, in_, 1.0 / n, EPS, ALU.mult, ALU.add))

            def norm(at, d, ffn):
                g0 = 2 * (d % 2)
                dve.wait_ge(taken, n_bank)
                link()
                dve.wait_ge(act_ops, at.act + 2)
                mean(mean_sq[:, 0:2], ss[:, 0:2], D)
                dve.wait_ge(act_ops, at.act + 3)
                link()
                op(dve.reciprocal(rstd[:, 0:2], root[:, 0:2]))
                link()
                if ffn:
                    dve.wait_ge(row_loaded, 16 * (d // 2 + 1))
                    if d:
                        dve.wait_ge(dve_rows, dve_rows_before(d - 1, 2) + ROWS)
                for t in range(2):
                    if ffn:
                        op(dve.scalar_tensor_tensor(h_ffn[:, t, :], x[:, g0 + t, :], rstd[:, t:t + 1], ffn_row[:, :],
                                                    ALU.mult, ALU.mult))
                    else:
                        op(dve.tensor_scalar(normed[:, t, :], x[:, g0 + t, :], rstd[:, t:t + 1], None, ALU.mult))

            def ple_norm(at, d):
                dve.wait_ge(sum_added, 2 * d + 2)
                norm(at, d, False)

            def ple_out(at, d, n):
                g0 = 2 * (d % 2)
                link()
                for t in range(2):
                    dve.wait_ge(evacs, at.evacs + t + 1)
                    take(dve.tensor_tensor(product[:, t, :], bank(), gates[:, n, t, :], ALU.mult))
                dve.wait_ge(taken, n_bank)
                for t in range(2):
                    xs = x[:, g0 + t, n * 512:(n + 1) * 512]
                    op(dve.tensor_tensor(xs, xs, product[:, t, :], ALU.add))

            def x_norm(at, d):
                norm(at, d, False)

            def nothing(at, d, *more):
                pass

            def conv_x(at, d, i):
                dve.wait_ge(evacs, WHERE[("conv_c", d, 1)].evacs + 2)
                for c in range(2):
                    take(dve.tensor_tensor(conv_u[:, 2 * i + c, 2:2 + HALF], bank(HALF), conv_cT[:, 2 * i + c, :],
                                           ALU.mult))

            def taps(at, d):
                if d % 2:
                    op(dve.tensor_copy(conv_u[:, :, 0:2], tail[:, :, :]))
                else:
                    op(dve.memset(conv_u[:, :, 0:2], 0.0))
                link()
                dve.wait_ge(taken, n_bank)
                for j in range(3):
                    for c in range(4):
                        u = conv_u[:, c, j:j + HALF]
                        if j == 0:
                            op(dve.tensor_scalar(ycT[:, c, :], u, col("conv", d // 2, c), None, ALU.mult))
                        else:
                            op(dve.scalar_tensor_tensor(ycT[:, c, :], u, col("conv", d // 2, 4 * j + c), ycT[:, c, :],
                                                        ALU.mult, ALU.add))
                    link()
                dve.wait_ge(evacs, at.evacs)
                op(dve.tensor_tensor(ycT, ycT, conv_bT, ALU.mult))
                op(dve.tensor_copy(tail[:, :, :], conv_u[:, :, HALF:HALF + 2]))

            def diff_norm(at, d):
                link()
                dve.wait_ge(evacs, at.evacs)
                flat = area_b[:, 0:2048]
                op(dve.tensor_tensor(squares, flat, flat, ALU.mult))
                link()
                op(dve.tensor_reduce(ss, squares.rearrange("p (g d) -> p g d", d=DHD), AX, ALU.add))
                link()
                mean(mean_sq, ss, DHD)
                dve.wait_ge(act_ops, at.act + 1)
                op(dve.reciprocal(rstd[:, :], root))
                link()
                groups = flat.rearrange("p (g d) -> p g d", d=DHD)
                op(dve.tensor_tensor(groups, groups, rstd[:, :].unsqueeze(2).to_broadcast([P, 32, DHD]), ALU.mult))

            def window(m, d, t):
                g = 2 * (d % 2) + t
                return m[:, 384 - g * P:512]

            def diff_scores(at, d, i):
                t, h = divmod(i, DH)
                b, w = i % 3, (2 * (d % 2) + t + 1) * P
                dve.wait_ge(evacs, WHERE[("diff_flip", d, i - 3)].evacs + 1 if i >= 3 else at.evacs)
                link()
                for m in range(2):
                    take(dve.scalar_tensor_tensor(diff_prob[b][:, m, 0:w], window(dist, d, t), SLOPES[h], bank(w),
                                                  ALU.mult, ALU.add))
                dve.wait_ge(taken, n_bank)
                for m in range(2):
                    op(dve.tensor_reduce(neg_top[:, b, m:m + 1], diff_prob[b][:, m, 0:w], AX, ALU.max, negate=True))

            def diff_flip(at, d, i):
                b, w = i % 3, (2 * (d % 2) + i // DH + 1) * P
                dve.wait_ge(act_ops, WHERE[("diff_scores", d, i)].act + 2)
                op(dve.reciprocal(inv[:, b, :], total[:, b, :]))
                link()
                p0, p1 = diff_prob[b][:, 0, 0:w], diff_prob[b][:, 1, 0:w]
                op(dve.tensor_scalar(inv_lam[:, b, 0:1], inv[:, b, 1:2], lam[:, d // 2, 3:4], None, ALU.mult))
                op(dve.tensor_scalar(p0, p0, inv[:, b, 0:1], None, ALU.mult))
                link()
                op(dve.scalar_tensor_tensor(p0, p1, inv_lam[:, b, 0:1], p0, ALU.mult, ALU.add))

            def diff_sub(at, d, t):
                y = area_y[:, t, :]
                dve.wait_ge(evacs, at.evacs)
                link()
                op(dve.tensor_tensor(scratch[:, :], y, y, ALU.mult))
                link()
                op(dve.tensor_reduce(ss[:, 0:4], scratch[:, :].rearrange("p (g d) -> p g d", d=P), AX, ALU.add))
                link()
                mean(mean_sq[:, 0:4], ss[:, 0:4], P)
                dve.wait_ge(act_ops, at.act + 1)
                op(dve.reciprocal(rstd[:, 0:4], root[:, 0:4]))
                link()
                heads = y.rearrange("p (h d) -> p h d", h=DH)
                op(dve.tensor_tensor(heads, heads, rstd[:, 0:4].unsqueeze(2).to_broadcast([P, DH, P]), ALU.mult))

            def mla_norm(at, d):
                dve.wait_ge(act_ops, at.act + 4)
                mean(mean_sq[:, 0:2], ss[:, 0:2], QL)
                mean(mean_sq[:, 2:4], ss[:, 2:4], KVL)
                dve.wait_ge(act_ops, at.act + 5)
                op(dve.reciprocal(rstd[:, 0:4], root[:, 0:4]))
                link()
                for i, (lo, hi) in enumerate(((0, QL), (QL, QL + KVL))):
                    part = latent[:, :, lo:hi]
                    r = rstd[:, 2 * i:2 * i + 2].unsqueeze(2).to_broadcast([P, 2, hi - lo])
                    op(dve.tensor_tensor(part, part, r, ALU.mult))

            def mla_qk(at, d):
                layer, g0 = d // 2, 2 * (d % 2)
                kr = latent[:, :, QL + KVL:LATENT]
                q16 = area_b[:, 0:1536].rearrange("p (g d) -> p g d", d=MQK)
                k16 = area_b[:, 1536:3072].rearrange("p (g d) -> p g d", d=MQK)[:, :, 0:MNOPE]
                gq, gk = mla_rows[:, layer, 0, :], mla_rows[:, layer, 1, :]
                sq = area_e[:, 0:1536].rearrange("p (g d) -> p g d", d=MQK)
                sk = area_e[:, 0:1024].rearrange("p (g d) -> p g d", d=MNOPE)
                dve.wait_ge(evacs, at.evacs)
                dve.wait_ge(act_ops, at.act)
                link()
                op(dve.tensor_tensor(sq, q16, q16, ALU.mult))
                link()
                op(dve.tensor_reduce(ss[:, 0:16], sq, AX, ALU.add))
                link()
                op(dve.tensor_tensor(sk, k16, k16, ALU.mult))
                link()
                op(dve.tensor_reduce(ss[:, 16:32], sk, AX, ALU.add))
                kr2 = scratch[:, 0:64].rearrange("p (t d) -> p t d", t=2)
                op(dve.tensor_tensor(kr2, kr, kr, ALU.mult))
                link()
                op(dve.tensor_reduce(ss_rope, kr2, AX, ALU.add))
                link()
                kss = ss[:, 16:32].rearrange("p (t h) -> p t h", t=2)
                op(dve.tensor_tensor(kss, kss, ss_rope.unsqueeze(2).to_broadcast([P, 2, MH]), ALU.add))
                link()
                mean(mean_sq, ss, MQK)
                dve.wait_ge(act_ops, at.act + 1)
                op(dve.reciprocal(rstd[:, :], root))
                link()
                op(dve.tensor_tensor(q16, q16, rstd[:, 0:16].unsqueeze(2).to_broadcast([P, 16, MQK]), ALU.mult))
                op(dve.tensor_tensor(k16, k16, rstd[:, 16:32].unsqueeze(2).to_broadcast([P, 16, MNOPE]), ALU.mult))
                link()
                op(dve.tensor_tensor(q16, q16, gq.unsqueeze(1).to_broadcast([P, 16, MQK]), ALU.mult))
                op(dve.tensor_tensor(k16, k16, gk[:, 0:MNOPE].unsqueeze(1).to_broadcast([P, 16, MNOPE]), ALU.mult))
                op(dve.tensor_tensor(kr, kr, gk[:, MNOPE:MQK].unsqueeze(1).to_broadcast([P, 2, MROPE]), ALU.mult))
                link()
                krs = scratch[:, 64:128].rearrange("p (t d) -> p t d", t=2)
                cos, sin = rope_cos[:, g0:g0 + 2, :], rope_sin[:, g0:g0 + 2, :]
                hr = MROPE // 2
                op(dve.tensor_tensor(krs[:, :, 0:hr], kr[:, :, hr:MROPE], sin[:, :, 0:hr], ALU.mult))
                op(dve.tensor_tensor(krs[:, :, hr:MROPE], kr[:, :, 0:hr], sin[:, :, hr:MROPE], ALU.mult))
                link()
                op(dve.tensor_tensor(kr, kr, cos, ALU.mult))
                link()
                op(dve.tensor_tensor(kr, kr, krs, ALU.add))
                link()
                for t in range(2):
                    r = rstd[:, 16 + MH * t:16 + MH * (t + 1)].unsqueeze(2).to_broadcast([P, MH, MROPE])
                    op(dve.tensor_tensor(km[:, t, :, MNOPE:MQK], kr[:, t, :].unsqueeze(1).to_broadcast([P, MH, MROPE]),
                                         r, ALU.mult))
                turned = scratch[:, :].rearrange("p (t h d) -> p t h d", t=2, h=MH)
                for t in range(2):
                    xr = qm[:, t, :, MNOPE:MQK]
                    s = rope_sin[:, g0 + t, :].unsqueeze(1).to_broadcast([P, MH, MROPE])
                    op(dve.tensor_tensor(turned[:, t, :, 0:hr], xr[:, :, hr:MROPE], s[:, :, 0:hr], ALU.mult))
                    op(dve.tensor_tensor(turned[:, t, :, hr:MROPE], xr[:, :, 0:hr], s[:, :, hr:MROPE], ALU.mult))
                link()
                for t in range(2):
                    xr = qm[:, t, :, MNOPE:MQK]
                    c = rope_cos[:, g0 + t, :].unsqueeze(1).to_broadcast([P, MH, MROPE])
                    op(dve.tensor_tensor(xr, xr, c, ALU.mult))
                link()
                for t in range(2):
                    xr = qm[:, t, :, MNOPE:MQK]
                    op(dve.tensor_tensor(xr, xr, turned[:, t, :, :], ALU.add))

            def mla_scores(at, d, i):
                t = i // MH
                b, w = i % 4, (2 * (d % 2) + t + 1) * P
                dve.wait_ge(evacs, WHERE[("mla_flip", d, i - 4)].evacs + 1 if i >= 4 else at.evacs)
                take(dve.tensor_tensor_reduce(mla_prob[b][:, 0:w], bank(w), window(mask, d, t), 1.0, LOWEST,
                                              ALU.add, ALU.max, top[:, b, 0:1]))
                dve.wait_ge(taken, n_bank)
                op(dve.tensor_scalar(neg_top[:, b, 0:1], top[:, b, 0:1], -1.0, None, ALU.mult))

            def mla_flip(at, d, i):
                b = i % 4
                dve.wait_ge(act_ops, WHERE[("mla_scores", d, i)].act + 1)
                op(dve.reciprocal(inv[:, b, 0:1], total[:, b, 0:1]))

            def mix(at, d, n, br):
                for t in range(2):
                    dve.wait_ge(evacs, at.evacs + t + 1)
                    s = gates[:, (3 * n + br) % 2, t, :]
                    if br == 0:
                        take(dve.tensor_tensor(mixed[:, t, n * 512:(n + 1) * 512], bank(), s, ALU.mult))
                    else:
                        if t == 0:
                            link()
                        take(dve.tensor_tensor(product[:, t, :], bank(), s, ALU.mult))
                if br:
                    dve.wait_ge(taken, n_bank)
                    for t in range(2):
                        m = mixed[:, t, n * 512:(n + 1) * 512]
                        op(dve.tensor_tensor(m, m, product[:, t, :], ALU.add))

            def out(at, d, n):
                for t in range(2):
                    xs = x[:, 2 * (d % 2) + t, n * 512:(n + 1) * 512]
                    take(dve.tensor_tensor(xs, bank(), xs, ALU.add))

            def ffn_norm(at, d):
                norm(at, d, True)

            def rank(at, d, i):
                dve.wait_ge(evacs, at.evacs)
                lists = [(key_scores[:, 4 * (i % 4) + 2 * t + c, :], top_v[:, t, 2 * i + c, :], top_i[:, t, 2 * i + c, :])
                         for t in range(2) for c in range(2)]
                for lo in (0, 8):
                    for values, v, n in lists:
                        op(dve.max(v[:, lo:lo + 8], values))
                    link()
                    for values, v, n in lists:
                        op(dve.max_index(n[:, lo:lo + 8], v[:, lo:lo + 8], values))
                    if lo == 0:
                        link()
                        for values, v, n in lists:
                            op(dve.match_replace(values, v[:, 0:8], values, LOWEST))
                        link()

            def topk(at, d, t, part):
                sums = cand.rearrange("p (h i j) -> p h i j", h=HEADS, i=TOPK)
                lists = cand.rearrange("p (h c) -> p h c", h=HEADS)[:, :, 0:CANDS]
                shape = [P, HEADS, TOPK, TOPK]
                link()
                if part == 0:
                    pair = top_v[:, t, :, :].rearrange("p (h c) k -> p h c k", c=2)
                    for lo, hi, js in ((0, 4, 16), (4, 16, 4)):
                        at0 = lo * 16
                        box = [P, HEADS, hi - lo, js]
                        op(dve.tensor_tensor(
                            lists[:, :, at0:at0 + (hi - lo) * js].rearrange("p h (i j) -> p h i j", j=js),
                            pair[:, :, 0, lo:hi].unsqueeze(3).to_broadcast(box),
                            pair[:, :, 1, 0:js].unsqueeze(2).to_broadcast(box), ALU.add))
                    op(dve.tensor_copy(top_f.rearrange("p h c k -> p (h c k)"), top_i[:, t, :, :].rearrange("p c k -> p (c k)")))
                elif part == 1:
                    for h in range(HEADS):
                        op(dve.max(best_v[:, h, 0:8], lists[:, h, :]))
                    link()
                    for h in range(HEADS):
                        op(dve.max_index(best_c[:, h, 0:8], best_v[:, h, 0:8], lists[:, h, :]))
                elif part == 2:
                    for h in range(HEADS):
                        op(dve.match_replace(lists[:, h, :], best_v[:, h, 0:8], lists[:, h, :], LOWEST))
                    link()
                    for h in range(HEADS):
                        op(dve.max(best_v[:, h, 8:16], lists[:, h, :]))
                elif part == 3:
                    for h in range(HEADS):
                        op(dve.max_index(best_c[:, h, 8:16], best_v[:, h, 8:16], lists[:, h, :]))
                    link()
                    number = best_c.rearrange("p h k -> p (h k)")
                    place = part_f.rearrange("p c h k -> p c (h k)")
                    by_16, by_4 = part_i[:, 0, :], part_i[:, 1, :]
                    op(dve.tensor_scalar(part_u[:, 0, :], number, 4, None, ALU.logical_shift_right))
                    op(dve.tensor_scalar(part_u[:, 1, :], number, 2, None, ALU.logical_shift_right))
                    op(dve.tensor_copy(by_16, number))
                    link()
                    op(dve.tensor_copy(place, part_u[:, :, :]))
                    link()
                    op(dve.scalar_tensor_tensor(place[:, 0, :], place[:, 1, :], -12.0, place[:, 0, :], ALU.add, ALU.max))
                    link()
                    op(dve.scalar_tensor_tensor(by_4, place[:, 0, :], -4.0, by_16, ALU.mult, ALU.add))
                    op(dve.scalar_tensor_tensor(by_16, place[:, 0, :], -16.0, by_16, ALU.mult, ALU.add))
                    link()
                    op(dve.scalar_tensor_tensor(place[:, 1, :], by_4, -48.0, by_16, ALU.add, ALU.max))
                elif part < 6:
                    c = part - 4
                    op(dve.tensor_tensor(sums, part_f[:, c, :, :].unsqueeze(3).to_broadcast(shape),
                                         iota[:, :].unsqueeze(1).unsqueeze(1).to_broadcast(shape), ALU.is_equal))
                    link()
                    op(dve.tensor_tensor(sums, sums, top_f[:, :, c, :].unsqueeze(2).to_broadcast(shape), ALU.mult))
                    link()
                    op(dve.tensor_reduce(part_i[:, c, :], cand.rearrange("p (g i) -> p g i", i=TOPK), AX, ALU.add))
                else:
                    dve.scalar_tensor_tensor(experts[:, d % 2, t, :], part_i[:, 0, :], 128.0, part_i[:, 1, :],
                                             ALU.mult, ALU.add).then_inc(experts_ready, 1)
                    op(dve.tensor_tensor(exps, best_v, best_v[:, :, 0:1].to_broadcast([P, HEADS, TOPK]),
                                         ALU.subtract))
                    dve.wait_ge(act_ops, at.act + 1)
                    op(dve.tensor_reduce(esum, exps, AX, ALU.add))
                    link()
                    op(dve.reciprocal(esum, esum))
                    link()
                    op(dve.tensor_tensor(gate[:, d % 2, t, :].rearrange("p (h k) -> p h k", h=HEADS), exps,
                                         esum.unsqueeze(2).to_broadcast([P, HEADS, TOPK]), ALU.mult))

            stage = dict(ple_norm=ple_norm, ple_out=ple_out, x_norm=x_norm, qkv=nothing, latent=nothing,
                         conv_c=nothing, conv_x=conv_x, conv_b=nothing, taps=taps, diff_norm=diff_norm,
                         diff_turn=nothing, diff_scores=diff_scores, diff_flip=diff_flip, diff_pv=nothing, diff_sub=diff_sub,
                         mla_norm=mla_norm, mla_up=nothing, mla_qk=mla_qk, mla_turn=nothing,
                         mla_scores=mla_scores, mla_flip=mla_flip, mla_pv=nothing, mla_out=nothing, mix_first=mix, mix_more=mix,
                         mix_turn=nothing, out=out, ffn_norm=ffn_norm, query=nothing, scores=nothing, rank=rank, topk=topk)
            rows = Rows()

            def use(step, phase, t, g, half):
                filled = turns_before(step, phase)
                pe_share = PE_SHARE[phase]
                dve_share = UNIT - pe_share
                for k in range(pe_share, UNIT):
                    r = half * UNIT + k
                    j = g * RING + r
                    column = slice(j, j + 1) if isinstance(g, int) else bass.ds(j, 1)
                    dve.wait_ge(landed[r], (g + (filled + 1)) * 16)
                    if PHASES[phase] == "U":
                        dve.scalar_tensor_tensor(ring[:, r, :], ring[:, r, :], 1.0, h_ffn[:, t, :], ALU.mult, ALU.mult,
                                                 accum_out=dots[:, column]).then_inc(dve_rows, 1)
                    else:
                        before = dve_rows_before(step, phase) + half * dve_share + k - pe_share
                        dve.wait_ge(dve_rows, g * (2 * dve_share) + before)
                        xs = x[:, 2 * (step % 2) + t, :]
                        dve.scalar_tensor_tensor(xs, ring[:, r, :], weight[:, column], xs, ALU.mult, ALU.add)\
                            .then_inc(dve_rows, 1)

            def serve(n):
                for phase, first, m in rows.parts(n):
                    step, t = rows.step, phase // 2
                    if first == 0:
                        link()
                        dve.wait_ge(taken, n_bank)
                        if PHASES[phase] == "V":
                            dve.wait_ge(weight_ready, 2 * step + t + 1)
                    for unit, groups in pieces(first, m):
                        if groups:
                            with dve.Fori(0, groups) as i:
                                use(step, phase, t, i + unit // 2, 0)
                                use(step, phase, t, i + unit // 2, 1)
                        else:
                            use(step, phase, t, unit // 2, unit % 2)
                    if first + m < UNITS:
                        continue
                    if PHASES[phase] == "U":
                        dve.wait_ge(gelu_ready, 2 * step + t + 1)
                        dve.tensor_tensor(weight[:, :], gate[:, step % 2, t, :], dots[:, :], ALU.mult)\
                            .then_inc(weight_ready, 1)
                    else:
                        dve.wait_ge(pe_rows, pe_rows_before(step, phase + 1))
                        dve.wait_ge(dve_rows, dve_rows_before(step, phase + 1))
                        xs = x[:, 2 * (step % 2) + t, :]
                        dve.tensor_tensor(xs, ps_sum[:, :, :].rearrange("p b n -> p (b n)"), xs, ALU.add)\
                            .then_inc(sum_added, 1)

            dve.wait_ge(consts_loaded, 16 * N_CONSTS)
            dve.wait_ge(consts_made, 5)
            products = scratch[:, 0:4 * DHD].rearrange("p (l c d) -> p l c d", l=DEPTH, c=2)
            n_setup = 0

            def make(ins):
                nonlocal n_setup
                ins.then_inc(setup_done, 1)
                n_setup += 1
                dve.wait_ge(setup_done, n_setup)
            pairs = lam_in.rearrange("p l (c two) d -> p l c two d", two=2)
            for layer in range(DEPTH):
                make(dve.tensor_tensor(products[:, layer, :, :], pairs[:, layer, :, 0, :], pairs[:, layer, :, 1, :], ALU.mult))
            for layer in range(DEPTH):
                make(dve.tensor_reduce(lam[:, layer, 0:2], products[:, layer, :, :], AX, ALU.add))
                make(dve.tensor_scalar(dq_gain[:, layer:layer + 1], col("g_dq", layer), float(DHD) ** -0.5, None, ALU.mult))
                make(dve.tensor_scalar(dsub_gain[:, layer:layer + 1], col("g_dsub", layer), 1.0 - LAMBDA_INIT[layer],
                                       None, ALU.mult))
            dve.memset(scratch[:, 0:1], 0.0).then_inc(consts_made, 1)
            dve.wait_ge(consts_made, 7)
            for layer in range(DEPTH):
                make(dve.tensor_tensor(lam[:, layer, 2:3], lam[:, layer, 1:2], lam[:, layer, 0:1], ALU.subtract))
                make(dve.tensor_scalar(lam[:, layer, 3:4], lam[:, layer, 2:3], LAMBDA_INIT[layer], None, ALU.subtract))
            for step, row, rest in PLAN:
                rows.step, rows.pos = step, 0
                for (name, d, *more), at, units in row:
                    assert (n_bank, n_op) == (at.taken, at.dve), (name, d, more, n_bank, n_op, at.taken, at.dve)
                    stage[name](at, d, *more)
                    serve(units)
                serve(rest)

        @block.tensor
        def _(pe):
            n_act = 0
            n_dve = 0
            n_tile = 0

            def act_bank(k=0):
                if n_act + k >= 3:
                    pe.wait_ge(evacs, n_act + k - 2)
                return ps_act[:, (n_act + k) % 3, :]

            def dve_bank(k=0):
                if n_dve + k >= 3:
                    pe.wait_ge(taken, n_dve + k - 2)
                return ps_dve[:, (n_dve + k) % 3, :]

            def to_act(ins):
                nonlocal n_act
                ins.then_inc(for_act, 1)
                n_act += 1

            def to_dve(ins):
                nonlocal n_dve
                ins.then_inc(for_dve, 1)
                n_dve += 1

            def tile(k=0):
                slot, use = (n_tile + k) % W_SLOTS, (n_tile + k) // W_SLOTS
                pe.wait_ge(w_loaded[slot], 16 * (use + 1))
                return wt[:, slot, :]

            def release(n):
                nonlocal n_tile
                n_tile += n

            def turn_tiles(source):
                b = act_bank()
                for t in range(2):
                    s = source(t)
                    ins = pe.transpose(b[0:s.shape[1], t * P:(t + 1) * P], s, ident[:, :])
                to_act(ins)

            def norm(at, d, source):
                pe.wait_ge(dve_ops, at.dve + 4)
                for k in range(KT):
                    turn_tiles(lambda t: source[:, t, k * P:(k + 1) * P])

            def rows_by_columns(lhsT, banks, width=512):
                last = []
                for kh in range(2):
                    w = tile(kh).rearrange("p (k n) -> p k n", k=4)
                    for t in range(2):
                        for k in range(4):
                            ins = pe.matmul(banks[t][:, 0:width], lhsT[:, 4 * kh + k, t * P:(t + 1) * P],
                                            w[:, k, 0:width], start=(kh + k == 0), stop=(kh == 1 and k == 3))
                        last.append(ins)
                last[1].then_inc(w_used, 1)
                return last[2:]

            def hT_ready(at):
                pe.wait_ge(evacs, at.evacs)

            def ple_norm(at, d):
                norm(at, d, normed)

            def ple_out(at, d, n):
                hT_ready(WHERE[("ple_out", d, 0)])
                for ins in rows_by_columns(hT, [act_bank(0), act_bank(1)]):
                    to_act(ins)
                pe.wait_ge(pT_loaded, 16 * (d + 1))
                w = tile(2).rearrange("p (k n) -> p k n", k=4)
                for t in range(2):
                    b = dve_bank()
                    for k in range(2):
                        ins = pe.matmul(b, pT[:, k, t * P:(t + 1) * P], w[:, k, :], start=(k == 0), stop=(k == 1))
                    to_dve(ins)
                release(3)

            def x_norm(at, d):
                norm(at, d, normed)

            def qkv(at, d, n):
                for ins in rows_by_columns(hT, [act_bank(0), act_bank(1)]):
                    to_act(ins)
                release(2)

            def latents(at, d):
                for ins in rows_by_columns(hT, [act_bank(0), act_bank(1)], LATENT):
                    to_act(ins)
                release(2)

            def columns_by_tokens(to, get_bank):
                w = tile().rearrange("p (k n) -> p k n", k=KT)
                for c in range(2):
                    b = get_bank()
                    for k in range(KT):
                        ins = pe.matmul(b[:, 0:HALF], w[:, k, c * P:(c + 1) * P], hT[:, k, :],
                                        start=(k == 0), stop=(k == KT - 1))
                    to(ins)
                release(1)

            def conv(at, d, i):
                hT_ready(WHERE[("conv_c", d, 0)])
                columns_by_tokens(to_act, act_bank)

            def conv_x(at, d, i):
                columns_by_tokens(to_dve, dve_bank)

            def nothing(at, d, *more):
                pass

            def diff_turn(at, d):
                pe.wait_ge(dve_ops, at.dve)
                for h in range(DH):
                    for c in range(2):
                        turn_tiles(lambda t: z[:, c, t, h * P:(h + 1) * P])

            def diff_scores(at, d, i):
                t, h = divmod(i, DH)
                w = (2 * (d % 2) + t + 1) * P
                pe.wait_ge(evacs, WHERE[("diff_turn", d)].evacs + 8)
                for m in range(2):
                    b = dve_bank()
                    lo, hi = m * DHD, (m + 1) * DHD
                    to_dve(pe.matmul(b[:, 0:w], diff_qT[lo:hi, h, t * P:(t + 1) * P], diff_kT[lo:hi, h, 0:w],
                                     start=True, stop=True))

            def flip(p, blocks):
                bank = act_bank()
                for k in range(blocks):
                    ins = pe.transpose(bank[:, k * P:(k + 1) * P], p[:, k * P:(k + 1) * P], ident[:, :])
                to_act(ins)

            def times_v(i, blocks, v, h, dv, flipped):
                bank = act_bank()
                pe.wait_ge(evacs, flipped + 1)
                for k in range(blocks):
                    ins = pe.matmul(bank[:, 0:dv], probT[:, i % 2, k, :], v[:, k, h * dv:(h + 1) * dv],
                                    start=(k == 0), stop=(k == blocks - 1))
                to_act(ins)

            def diff_flip(at, d, i):
                pe.wait_ge(dve_ops, at.dve + 4)
                flip(diff_prob[i % 3][:, 0, :], 2 * (d % 2) + i // DH + 1)

            def diff_pv(at, d, i):
                t, h = divmod(i, DH)
                times_v(i, 2 * (d % 2) + t + 1, diff_v, h, P, WHERE[("diff_flip", d, i)].evacs)

            def turn_rows(t):
                bank = act_bank()
                for k in range(4):
                    ins = pe.transpose(bank[:, k * P:(k + 1) * P], area_y[:, t, k * P:(k + 1) * P], ident[:, :])
                to_act(ins)

            def diff_sub(at, d, t):
                pe.wait_ge(dve_ops, at.dve + 5)
                turn_rows(t)

            def mla_norm(at, d):
                pe.wait_ge(dve_ops, at.dve + 5)
                for k in range(3):
                    turn_tiles(lambda t: latent[:, t, k * P:(k + 1) * P])

            def mla_up(at, d):
                pe.wait_ge(evacs, at.evacs)
                uq = tile(0)[:, 0:1536].rearrange("p (k n) -> p k n", k=2)
                ukv = tile(1)
                for t in range(2):
                    ts = slice(t * P, (t + 1) * P)
                    for lo, hi in ((0, 512), (512, 768)):
                        b = act_bank()
                        for k in range(2):
                            ins = pe.matmul(b[:, 0:hi - lo], cqT[:, k, ts], uq[:, k, lo:hi], start=(k == 0), stop=(k == 1))
                        to_act(ins)
                    for i in range(2):
                        to_act(pe.matmul(act_bank(), ckvT[:, ts], ukv[:, 512 * i:512 * (i + 1)], start=True, stop=True))
                release(2)

            def mla_turn(at, d):
                pe.wait_ge(dve_ops, at.dve)
                for h in range(MH):
                    for source in (qm, km):
                        turn_tiles(lambda t: source[:, t, h, :])

            def mla_scores(at, d, i):
                t, h = divmod(i, MH)
                w = (2 * (d % 2) + t + 1) * P
                pe.wait_ge(evacs, WHERE[("mla_turn", d)].evacs + 16)
                b = dve_bank()
                to_dve(pe.matmul(b[:, 0:w], mla_qT[0:MQK, h, t * P:(t + 1) * P], mla_kT[0:MQK, h, 0:w],
                                 start=True, stop=True))

            def mla_flip(at, d, i):
                pe.wait_ge(act_ops, WHERE[("mla_scores", d, i)].act + 1)
                flip(mla_prob[i % 4], 2 * (d % 2) + i // MH + 1)

            def mla_pv(at, d, i):
                t, h = divmod(i, MH)
                times_v(i, 2 * (d % 2) + t + 1, mla_v, h, MV, WHERE[("mla_flip", d, i)].evacs)

            def mla_out(at, d, t):
                pe.wait_ge(evacs, at.evacs)
                turn_rows(t)

            def mix(at, d, n, br):
                for ins in rows_by_columns(hT, [act_bank(0), act_bank(1)]):
                    to_act(ins)
                w = tile(2).rearrange("p (k n) -> p k n", k=4)
                if br == 1:
                    pe.wait_ge(evacs, WHERE[("mla_out", d, 1)].evacs + 1)
                if br == 0:
                    pe.wait_ge(evacs, WHERE[("diff_sub", d, 1)].evacs + 1)
                if br == 2:
                    pe.wait_ge(dve_ops, WHERE[("taps", d)].dve + 15)
                for t in range(2):
                    b = dve_bank()
                    for k in range(4):
                        ins = pe.matmul(b, (ydT, ymT, ycT)[br][:, k, t * P:(t + 1) * P], w[:, k, :],
                                        start=(k == 0), stop=(k == 3))
                    to_dve(ins)
                release(3)

            def mix_turn(at, d):
                pe.wait_ge(dve_ops, at.dve)
                for k in range(KT):
                    turn_tiles(lambda t: mixed[:, t, k * P:(k + 1) * P])

            def out(at, d, n):
                pe.wait_ge(evacs, at.evacs)
                for ins in rows_by_columns(mixedT, [dve_bank(0), dve_bank(1)]):
                    to_dve(ins)
                release(2)

            def ffn_norm(at, d):
                norm(at, d, h_ffn)

            def query(at, d, i):
                hT_ready(WHERE[("query", d, 0)])
                columns_by_tokens(to_act, act_bank)

            def scores(at, d, i):
                pe.wait_ge(evacs, WHERE[("query", d, i)].evacs + 2)
                pe.wait_ge(keys_loaded, 32 * (d + 1))
                for t in range(2):
                    b = act_bank()
                    for c in range(2):
                        half, at_key = divmod((2 * i + c) * P, 1024)
                        ins = pe.matmul(b[:, c * P:(c + 1) * P], queryT[:, 2 * i + c, t * P:(t + 1) * P],
                                        sub_keys[half][:, at_key:at_key + P], start=True, stop=True)
                    to_act(ins)

            stage = dict(ple_norm=ple_norm, ple_out=ple_out, x_norm=x_norm, qkv=qkv, latent=latents, conv_c=conv,
                         conv_x=conv_x, conv_b=conv, taps=nothing, diff_norm=nothing, diff_turn=diff_turn,
                         diff_scores=diff_scores, diff_flip=diff_flip, diff_pv=diff_pv, diff_sub=diff_sub, mla_norm=mla_norm,
                         mla_up=mla_up, mla_qk=nothing, mla_turn=mla_turn, mla_scores=mla_scores,
                         mla_flip=mla_flip, mla_pv=mla_pv, mla_out=mla_out, mix_first=mix, mix_more=mix, mix_turn=mix_turn,
                         out=out, ffn_norm=ffn_norm, query=query, scores=scores, rank=nothing, topk=nothing)
            rows = Rows()

            def add_rows(step, phase, g, half):
                filled = turns_before(step, phase)
                single = isinstance(g, int)
                share = PE_SHARE[phase]
                for k in range(share):
                    r, i = half * UNIT + k, half * share + k
                    begin = single and g == 0 and i == 0
                    end = single and g == GROUPS - 1 and i == 2 * share - 1
                    pe.wait_ge(diag_ready, g * (2 * share) + (pe_rows_before(step, phase) + i + 1))
                    pe.wait_ge(landed[r], (g + (filled + 1)) * 16)
                    for b in range(2):
                        ins = pe.matmul(ps_sum[:, b, :], diag[:, i, :], ring[:, r, b * 512:(b + 1) * 512],
                                        start=begin, stop=end)
                    ins.then_inc(pe_rows, 1)

            def serve(n):
                for phase, first, m in rows.parts(n):
                    step = rows.step
                    if PHASES[phase] == "U":
                        continue
                    if first == 0 and 2 * step + phase // 2:
                        pe.wait_ge(sum_added, 2 * step + phase // 2)
                    for unit, groups in pieces(first, m):
                        if groups:
                            with pe.Fori(0, groups) as i:
                                add_rows(step, phase, i + unit // 2, 0)
                                add_rows(step, phase, i + unit // 2, 1)
                        else:
                            add_rows(step, phase, unit // 2, unit % 2)

            pe.wait_ge(consts_loaded, 16 * N_CONSTS)
            for step, row, rest in PLAN:
                rows.step, rows.pos = step, 0
                for (name, d, *more), at, units in row:
                    assert (n_act, n_dve, n_tile) == (at.evacs, at.taken, at.tile), (name, d, more)
                    stage[name](at, d, *more)
                    serve(units)
                serve(rest)


def _tiles(w, k, n):
    kk, nn = w.shape[0] // (k * P), w.shape[1] // n
    return w.reshape(kk, k, P, nn, n).transpose(0, 3, 2, 1, 4).reshape(kk, nn, P, k * n)


def _layer_weights(w, layer):
    out = np.zeros((NT_PLE + NT_DENSE, P, 2048), np.float32)
    at = 0

    def put(tile):
        nonlocal at
        out[at, :, :tile.shape[1]] = tile
        at += 1

    def by_rows(m, n):
        for kh in range(2):
            put(_tiles(m, 4, 512)[kh, n])

    for n in range(2):
        by_rows(w["w_ple_gate"][layer], n)
        put(_tiles(w["w_ple_proj"][layer], 2, 512)[0, n])
    w_in = w["w_in"][layer]
    first = 1536 + LATENT
    for part in (1, 2, 0):
        cut = _tiles(w_in[:, first + 512 * part:first + 512 * (part + 1)], KT, 256)
        put(cut[0, 0])
        put(cut[0, 1])
    for n in range(3):
        by_rows(w_in[:, 0:1536], n)
    lat = np.zeros((D, 512), np.float32)
    lat[:, :LATENT] = w_in[:, 1536:1536 + LATENT]
    by_rows(lat, 0)
    first += 3 * 512
    put(_tiles(w["w_uq"][layer], 2, 768)[0, 0])
    put(w["w_ukv"][layer])
    for n in range(2):
        for br, name in enumerate(("w_br_diff", "w_br_mla", "w_br_conv")):
            by_rows(w_in[:, first + D * br:first + D * (br + 1)], n)
            put(_tiles(w[name][layer], 4, 512)[0, n])
    for n in range(2):
        by_rows(w["w_out"][layer], n)
    cut = _tiles(w["w_query"][layer], KT, 256)
    for i in range(HP // 2):
        put(cut[0, i])
    assert at == len(out)
    return out


def _layer_columns(w, layer):
    def split(v):
        return v.reshape(-1, P).T

    return np.concatenate([
        split(w["g_mix"][layer]), split(w["g_ple"][layer]),
        np.tile(w["g_diff_q"][layer], 2)[:, None], np.tile(w["g_diff_k"][layer], 2)[:, None],
        w["g_diff_sub"][layer][:, None], split(w["g_cq"][layer]), split(w["g_ckv"][layer]),
        w["conv_w"][layer].reshape(-1, P).T], axis=1)


def _everywhere(v):
    return np.ascontiguousarray(np.broadcast_to(v, (P, *v.shape)))


def kernel(**inputs):
    from concourse import bacc
    from concourse.bass_utils import run_bass_kernel_spmd

    w = {k: np.asarray(v) for k, v in inputs.items()}
    half = MROPE // 2
    angle = np.arange(SEQ, dtype=np.float32)[:, None] * (
        10000.0 ** (-np.arange(half, dtype=np.float32) / half)).astype(np.float32)[None, :]
    cos = np.concatenate([np.cos(angle), np.cos(angle)], axis=1)
    sin = np.concatenate([-np.sin(angle), np.sin(angle)], axis=1)
    arrays = {
        "x": w["x"].reshape(4, P, D),
        "pT": w["p"].reshape(DEPTH, SEQ, 2, P).transpose(0, 3, 2, 1),
        "weights": np.stack([_layer_weights(w, layer) for layer in range(DEPTH)]),
        "keys": w["sub_keys"].reshape(DEPTH, 2, 2, HEADS // 2, P, P).transpose(0, 2, 5, 3, 1, 4)
        .reshape(DEPTH, 2, P, HEADS * P),
        "cols": np.stack([_layer_columns(w, layer) for layer in range(DEPTH)], axis=1),
        "ffn_rows": np.stack([_everywhere(w["g_ffn"][layer]) for layer in range(DEPTH)]),
        "mla_rows": _everywhere(np.stack([w["g_mla_q"], w["g_mla_k"]], axis=1)),
        "lam": _everywhere(np.stack([w["lam_q1"], w["lam_k1"], w["lam_q2"], w["lam_k2"]], axis=1)),
        "rope": np.stack([cos, sin]).reshape(2, 4, P, MROPE).transpose(0, 2, 1, 3).astype(np.float32),
        "ident": np.eye(P, dtype=np.float32),
        **{f"u{layer}": w["u_experts"][layer] for layer in range(DEPTH)},
        **{f"v{layer}": w["v_experts"][layer] for layer in range(DEPTH)},
    }
    arrays = {"in_" + k: np.ascontiguousarray(v) for k, v in arrays.items()}
    nc = bacc.Bacc("TRN2", target_bir_lowering=False, num_devices=1)
    aps = {k[3:]: nc.dram_tensor(k, v.shape, F32, kind="ExternalInput").ap() for k, v in arrays.items()}
    aps["out"] = nc.dram_tensor("out_x", (4, P, D), F32, kind="ExternalOutput").ap()
    trunk(nc, aps)
    r = run_bass_kernel_spmd(nc, [arrays], core_ids=[0])
    return r.results[0]["out_x"].reshape(1, SEQ, D)
```
